# Optimizing a Trainium2 kernel written in Bass

```python
import math
import jax
import jax.numpy as jnp
from jax import lax
import numpy as np

D_MODEL = 1024
BATCH = 1
SEQ = 1024
DEPTH = 1

GRID_W = 64
CTX_LEN = 256
D_MIX = D_MODEL
D_HYENA = D_MIX // 2
HYENA_SHORT_W = 3
FILTER_ORDER = 64
POS_EMB_DIM = 33
DECAY_TARGET = 1e-2
FAST_DECAY_PCT = 0.3
SLOW_DECAY_PCT = 1.5
MIN_DECAY = math.log(DECAY_TARGET) / FAST_DECAY_PCT
MAX_DECAY = math.log(DECAY_TARGET) / SLOW_DECAY_PCT
NOPE_DIM = 128
ROPE_DIM = 64
QK_DIM = NOPE_DIM + ROPE_DIM
V_DIM = 128
MLA_HEADS = (D_MIX - D_HYENA) // V_DIM
Q_RANK = 256
KV_RANK = 128
ROPE_THETA = 10000.0
Q_BLOCK = 128
N_EXPERTS = 32
TOP_K = 4
D_FF = D_MODEL
SWIGLU_ALPHA = 1.702
SWIGLU_LIMIT = 7.0
MOE_BLOCK = 128
NORM_EPS = 1e-6
HY_COLS = 3 * D_HYENA
KV_COL = HY_COLS + Q_RANK
PE_COL = KV_COL + KV_RANK
IN_COLS = PE_COL + ROPE_DIM

kernel_name = "hyena_mla_moe_hybrid_dit_layer"

def rms_norm(x, g):
    xf = x.astype(jnp.float32)
    y = xf * lax.rsqrt(jnp.mean(xf * xf, axis=-1, keepdims=True) + NORM_EPS)
    return (y * g.astype(jnp.float32)).astype(x.dtype)

def modulate(h, shift, scale):
    return h * (1.0 + scale) + shift

def axial_rope_tables(L):
    rows = L // GRID_W
    row = jnp.repeat(jnp.arange(rows, dtype=jnp.int32), GRID_W).astype(jnp.float32)
    col = jnp.tile(jnp.arange(GRID_W, dtype=jnp.int32), rows).astype(jnp.float32)
    n_freq = ROPE_DIM // 4
    inv_freq = jnp.power(ROPE_THETA, -jnp.arange(n_freq, dtype=jnp.float32) / n_freq)
    ang = jnp.stack([row[:, None] * inv_freq, col[:, None] * inv_freq], axis=1)
    return jnp.cos(ang), jnp.sin(ang)

def apply_axial_rope(x, cos, sin):
    shp = x.shape
    xr = x.reshape(*shp[:-1], 2, ROPE_DIM // 2)
    x1, x2 = xr[..., : ROPE_DIM // 4], xr[..., ROPE_DIM // 4:]
    cb = cos[None, :, None].astype(x.dtype)
    sb = sin[None, :, None].astype(x.dtype)
    out = jnp.concatenate([x1 * cb - x2 * sb, x2 * cb + x1 * sb], axis=-1)
    return out.reshape(shp)

def short_conv(u, w, b):
    up = jnp.pad(u, ((0, 0), (1, 1), (0, 0)))
    return up[:, :-2] * w[0] + up[:, 1:-1] * w[1] + up[:, 2:] * w[2] + b

def hyena_filters(L, w1, b1, w2, b2, w3, b3, w4, freq):
    t = jnp.linspace(0.0, 1.0, L, dtype=jnp.float32)[:, None]
    bands = (POS_EMB_DIM - 1) // 2
    w_ang = 2.0 * math.pi * jnp.arange(L, dtype=jnp.float32)[:, None] / L
    f = jnp.linspace(1e-4, bands - 1, bands, dtype=jnp.float32)[None, :]
    z = jnp.concatenate([t, jnp.cos(f * w_ang), -jnp.sin(f * w_ang)], axis=-1)
    fr = freq.astype(jnp.float32)
    h = jnp.sin(fr * (z @ w1.astype(jnp.float32) + b1.astype(jnp.float32)))
    h = jnp.sin(fr * (h @ w2.astype(jnp.float32) + b2.astype(jnp.float32)))
    h = jnp.sin(fr * (h @ w3.astype(jnp.float32) + b3.astype(jnp.float32)))
    h = (h @ w4.astype(jnp.float32)).reshape(L, 2, D_HYENA)
    deltas = jnp.linspace(MIN_DECAY, MAX_DECAY, D_HYENA, dtype=jnp.float32)
    decay = jnp.exp(-t * jnp.abs(deltas))
    h = h * decay[:, None, :]
    h = h / jnp.sum(jnp.abs(h), axis=(0, 1), keepdims=True)
    return h[:, 0], h[:, 1]

def bidir_fft_conv(u, h_fwd, h_bwd):
    B, L, C = u.shape
    kern = jnp.concatenate([h_fwd, jnp.zeros((1, C), h_fwd.dtype), h_bwd[:0:-1]], axis=0)
    k_f = jnp.fft.rfft(kern, n=2 * L, axis=0)
    u_f = jnp.fft.rfft(u.astype(jnp.float32), n=2 * L, axis=1)
    y = jnp.fft.irfft(u_f * k_f[None], n=2 * L, axis=1)[:, :L]
    return y.astype(u.dtype)

def hyena_mixer(u, conv_w, conv_b, w1, b1, w2, b2, w3, b3, w4, freq, bias):
    L = u.shape[1]
    uc = short_conv(u, conv_w, conv_b)
    x0, x1, v = jnp.split(uc, 3, axis=-1)
    h_fwd, h_bwd = hyena_filters(L, w1, b1, w2, b2, w3, b3, w4, freq)
    v = v * x1
    v = bidir_fft_conv(v, h_fwd, h_bwd) + v * bias
    return v * x0

def mla_queries(c_q, q_norm_g, w_uq, qn_g, rope):
    B, L, _ = c_q.shape
    q = (rms_norm(c_q, q_norm_g) @ w_uq).reshape(B, L, MLA_HEADS, QK_DIM)
    q = rms_norm(q, qn_g)
    if rope is not None:
        q = jnp.concatenate([q[..., :NOPE_DIM], apply_axial_rope(q[..., NOPE_DIM:], *rope)], axis=-1)
    return q

def mla_keys_values(c_kv, k_pe, kv_norm_g, w_ukv, kn_g, rope):
    B, L, _ = c_kv.shape
    kv = (rms_norm(c_kv, kv_norm_g) @ w_ukv).reshape(B, L, MLA_HEADS, NOPE_DIM + V_DIM)
    k_nope, v = jnp.split(kv, [NOPE_DIM], axis=-1)
    k_rope = jnp.broadcast_to(k_pe[:, :, None, :], (B, L, MLA_HEADS, ROPE_DIM))
    k = rms_norm(jnp.concatenate([k_nope, k_rope], axis=-1), kn_g)
    if rope is not None:
        k = jnp.concatenate([k[..., :NOPE_DIM], apply_axial_rope(k[..., NOPE_DIM:], *rope)], axis=-1)
    return k, v

def block_attention(q, k, v):
    B, Lq, H, _ = q.shape
    n_blk = Lq // Q_BLOCK
    q_blocks = q.reshape(B, n_blk, Q_BLOCK, H, QK_DIM).transpose(1, 0, 2, 3, 4)
    scale = QK_DIM ** -0.5

    def one_block(qb):
        s = jnp.einsum('bqhd,bkhd->bhqk', qb, k, preferred_element_type=jnp.float32) * scale
        p = jax.nn.softmax(s, axis=-1)
        return jnp.einsum('bhqk,bkhd->bqhd', p.astype(v.dtype), v)

    out = lax.map(one_block, q_blocks)
    return out.transpose(1, 0, 2, 3, 4).reshape(B, Lq, H * V_DIM)

def moe_ffn(h, router_w, router_b, w_gu, b_gu, w_down, b_down):
    T, D = h.shape
    logits = (h @ router_w + router_b).astype(jnp.float32)
    top_logits, top_idx = lax.top_k(logits, TOP_K)
    gates = jax.nn.softmax(top_logits, axis=-1)
    n_pairs = T * TOP_K
    flat_e = top_idx.reshape(-1)
    flat_tok = jnp.repeat(jnp.arange(T, dtype=jnp.int32), TOP_K)
    flat_gate = gates.reshape(-1)
    order = jnp.argsort(flat_e)
    sorted_e = flat_e[order]
    counts = jnp.bincount(flat_e, length=N_EXPERTS)
    starts = jnp.cumsum(counts) - counts
    padded = (counts + MOE_BLOCK - 1) // MOE_BLOCK * MOE_BLOCK
    padded_ends = jnp.cumsum(padded)
    padded_starts = padded_ends - padded
    dest = padded_starts[sorted_e] + jnp.arange(n_pairs, dtype=jnp.int32) - starts[sorted_e]
    n_blocks = -(-n_pairs // MOE_BLOCK) + N_EXPERTS
    n_rows = n_blocks * MOE_BLOCK
    row_tok = jnp.full((n_rows,), T, jnp.int32).at[dest].set(flat_tok[order])
    row_gate = jnp.zeros((n_rows,), jnp.float32).at[dest].set(flat_gate[order])
    block_start = jnp.arange(n_blocks, dtype=jnp.int32) * MOE_BLOCK
    block_e = jnp.minimum(jnp.searchsorted(padded_ends, block_start, side='right'), N_EXPERTS - 1)
    h_pad = jnp.concatenate([h, jnp.zeros((1, D), h.dtype)], axis=0)
    xs = h_pad[row_tok].reshape(n_blocks, MOE_BLOCK, D)

    def expert_block(args):
        xb, e = args
        gu = xb @ w_gu[e] + b_gu[e]
        gate, up = jnp.split(gu, 2, axis=-1)
        gate = jnp.minimum(gate, SWIGLU_LIMIT)
        up = jnp.clip(up, -SWIGLU_LIMIT, SWIGLU_LIMIT)
        glu = gate * jax.nn.sigmoid(SWIGLU_ALPHA * gate)
        return ((up + 1.0) * glu) @ w_down[e] + b_down[e]

    ys = lax.map(expert_block, (xs, block_e)).reshape(n_rows, D)
    out = jax.ops.segment_sum(ys * row_gate[:, None], row_tok, num_segments=T + 1)[:T]
    return out.astype(h.dtype)

def setup_inputs(seed: int = 0) -> dict:
    key = jax.random.key(seed)
    ks = iter(jax.random.split(key, 40))

    def nrm(shape, scale):
        return scale * jax.random.normal(next(ks), shape, jnp.float32)

    def gain(shape):
        return 1.0 + nrm(shape, 0.02)

    L = DEPTH
    return {
        "x": nrm((BATCH, SEQ, D_MODEL), 1.0),
        "c": nrm((BATCH, D_MODEL), 1.0),
        "ctx": nrm((BATCH, CTX_LEN, D_MODEL), 1.0),
        "c_ctx": nrm((D_MODEL,), 1.0),
        "mod_w": nrm((L, D_MODEL, 6 * D_MODEL), D_MODEL ** -0.5),
        "mod_b": nrm((L, 6 * D_MODEL), 0.02),
        "norm1_g": gain((L, D_MODEL)),
        "w_in": nrm((L, D_MODEL, IN_COLS), D_MODEL ** -0.5),
        "hy_conv_w": nrm((L, HYENA_SHORT_W, HY_COLS), HYENA_SHORT_W ** -0.5),
        "hy_conv_b": nrm((L, HY_COLS), 0.02),
        "hy_f_w1": nrm((L, POS_EMB_DIM, FILTER_ORDER), POS_EMB_DIM ** -0.5),
        "hy_f_b1": nrm((L, FILTER_ORDER), 0.02),
        "hy_f_w2": nrm((L, FILTER_ORDER, FILTER_ORDER), FILTER_ORDER ** -0.5),
        "hy_f_b2": nrm((L, FILTER_ORDER), 0.02),
        "hy_f_w3": nrm((L, FILTER_ORDER, FILTER_ORDER), FILTER_ORDER ** -0.5),
        "hy_f_b3": nrm((L, FILTER_ORDER), 0.02),
        "hy_f_w4": nrm((L, FILTER_ORDER, 2 * D_HYENA), FILTER_ORDER ** -0.5),
        "hy_f_freq": gain((L, FILTER_ORDER)),
        "hy_bias": nrm((L, D_HYENA), 1.0),
        "mla_q_norm_g": gain((L, Q_RANK)),
        "mla_w_uq": nrm((L, Q_RANK, MLA_HEADS * QK_DIM), Q_RANK ** -0.5),
        "mla_kv_norm_g": gain((L, KV_RANK)),
        "mla_w_ukv": nrm((L, KV_RANK, MLA_HEADS * (NOPE_DIM + V_DIM)), KV_RANK ** -0.5),
        "qk_norm_q_g": gain((L, QK_DIM)),
        "qk_norm_k_g": gain((L, QK_DIM)),
        "w_out": nrm((L, D_MIX, D_MODEL), D_MIX ** -0.5),
        "norm2_g": gain((L, D_MODEL)),
        "router_w": nrm((L, D_MODEL, N_EXPERTS), D_MODEL ** -0.5),
        "router_b": nrm((L, N_EXPERTS), 0.01),
        "exp_w_gu": nrm((L, N_EXPERTS, D_MODEL, 2 * D_FF), D_MODEL ** -0.5),
        "exp_b_gu": nrm((L, N_EXPERTS, 2 * D_FF), 0.02),
        "exp_w_down": nrm((L, N_EXPERTS, D_FF, D_MODEL), D_FF ** -0.5),
        "exp_b_down": nrm((L, N_EXPERTS, D_MODEL), 0.02),
    }

def reference(x, c, ctx, c_ctx, mod_w, mod_b, norm1_g, w_in, hy_conv_w, hy_conv_b,
              hy_f_w1, hy_f_b1, hy_f_w2, hy_f_b2, hy_f_w3, hy_f_b3, hy_f_w4, hy_f_freq, hy_bias,
              mla_q_norm_g, mla_w_uq, mla_kv_norm_g, mla_w_ukv, qk_norm_q_g, qk_norm_k_g,
              w_out, norm2_g, router_w, router_b, exp_w_gu, exp_b_gu, exp_w_down, exp_b_down):
    rope = axial_rope_tables(x.shape[1])
    xc = ctx
    for layer in range(DEPTH):
        last = layer == DEPTH - 1
        mod = jax.nn.silu(c) @ mod_w[layer] + mod_b[layer]
        sh1, sc1, g1, sh2, sc2, g2 = jnp.split(mod[:, None, :], 6, axis=-1)
        mod_c = jax.nn.silu(c_ctx) @ mod_w[layer] + mod_b[layer]
        csh1, csc1, cg1, csh2, csc2, cg2 = jnp.split(mod_c, 6, axis=-1)
        hy_p = (hy_conv_w[layer], hy_conv_b[layer], hy_f_w1[layer], hy_f_b1[layer],
                hy_f_w2[layer], hy_f_b2[layer], hy_f_w3[layer], hy_f_b3[layer],
                hy_f_w4[layer], hy_f_freq[layer], hy_bias[layer])
        q_p = (mla_q_norm_g[layer], mla_w_uq[layer], qk_norm_q_g[layer])
        kv_p = (mla_kv_norm_g[layer], mla_w_ukv[layer], qk_norm_k_g[layer])
        moe_p = (router_w[layer], router_b[layer], exp_w_gu[layer], exp_b_gu[layer],
                 exp_w_down[layer], exp_b_down[layer])
        w_in_l = w_in[layer]

        hc = modulate(rms_norm(xc, norm1_g[layer]), csh1, csc1)
        if last:
            ckv_c, kpe_c = jnp.split(hc @ w_in_l[:, KV_COL:], [KV_RANK], axis=-1)
        else:
            hy_c, cq_c, ckv_c, kpe_c = jnp.split(hc @ w_in_l, [HY_COLS, KV_COL, PE_COL], axis=-1)
        k_c, v_c = mla_keys_values(ckv_c, kpe_c, *kv_p, rope=None)

        h = modulate(rms_norm(x, norm1_g[layer]), sh1, sc1)
        hy, cq, ckv, kpe = jnp.split(h @ w_in_l, [HY_COLS, KV_COL, PE_COL], axis=-1)
        y_hy = hyena_mixer(hy, *hy_p)
        q = mla_queries(cq, *q_p, rope=rope)
        k, v = mla_keys_values(ckv, kpe, *kv_p, rope=rope)
        y_att = block_attention(q, jnp.concatenate([k, k_c], axis=1),
                                jnp.concatenate([v, v_c], axis=1))
        x_new = x + g1 * (jnp.concatenate([y_hy, y_att], axis=-1) @ w_out[layer])
        h2 = modulate(rms_norm(x_new, norm2_g[layer]), sh2, sc2)
        x_new = x_new + g2 * moe_ffn(h2.reshape(-1, D_MODEL), *moe_p).reshape(x.shape)

        if not last:
            yc_hy = hyena_mixer(hy_c, *hy_p)
            q_c = mla_queries(cq_c, *q_p, rope=None)
            yc_att = block_attention(q_c, k_c, v_c)
            xc = xc + cg1 * (jnp.concatenate([yc_hy, yc_att], axis=-1) @ w_out[layer])
            h2c = modulate(rms_norm(xc, norm2_g[layer]), csh2, csc2)
            xc = xc + cg2 * moe_ffn(h2c.reshape(-1, D_MODEL), *moe_p).reshape(xc.shape)
        x = x_new
    return x


_drawn_inputs = setup_inputs


def setup_inputs(seed=0):
    import zlib

    import numpy as np

    out = dict(_drawn_inputs(seed))
    spreads = {}
    factors = {'ctx': 3.191,
     'hy_f_b1': 6.312,
     'hy_f_b2': 5.015,
     'hy_f_b3': 10.776,
     'hy_f_freq': 8.0,
     'mla_q_norm_g': 8.0,
     'mla_kv_norm_g': 4.192,
     'qk_norm_q_g': 8.0,
     'qk_norm_k_g': 8.0,
     'router_b': 9.21,
     'exp_b_gu': 7.413,
     'exp_b_down': 28.338,
     'hy_conv_b': 3.418,
     'norm2_g': 3.093}
    for name, (base, spread) in spreads.items():
        noise = np.random.default_rng([zlib.crc32(name.encode()), seed]).standard_normal(out[name].shape)
        drawn = base * np.exp(spread * noise) if base else spread * noise
        out[name] = jnp.asarray(drawn.astype(out[name].dtype))
    for name, factor in factors.items():
        out[name] = (out[name] * factor).astype(out[name].dtype)
    return out
```

```python
import math
from contextlib import ExitStack

import numpy as np
import concourse.bass as bass
from concourse import mybir

F32 = mybir.dt.float32
I32 = mybir.dt.int32
ALU = mybir.AluOpType
ACT = mybir.ActivationFunctionType
X = mybir.AxisListType.X

P = 128
D = 1024
DT = D // P
T = 1024
TT = T // P
CTX = 256
CT = CTX // P
KT = TT + CT
KEYS = T + CTX
HY = 512
HC = HY // P
NH = 4
NOPE, ROPE, VD = 128, 64, 128
QK = NOPE + ROPE
QR, KR = 256, 128
LAT = QR + KR + ROPE
INC = 3 * HY + LAT
NE, TOPK, FF = 32, 4, 1024
EPS = 1e-6
SCALE = QK ** -0.5
PAIRS = T * TOPK
CAP = T
BLK = 512
NB = BLK // P
LCOL = CAP // P
NOPAIR = 4 * PAIRS
MAGIC = 1.5 * 2.0 ** 23
GRID_W, THETA = 64, 10000.0

FACTORS = [(3 * math.pi / 4 / 256, 2 * math.pi / 256, 256, 4),
           (math.pi / 4 / 256, 2 * math.pi / 256, 256, 4),
           (math.pi / 512, 2 * math.pi / 512, 256, 4),
           (math.pi / 256, 2 * math.pi / 256, 128, 2),
           (0.0, 2 * math.pi / 256, 128, 2)]
PAIR_TILES = [(0, 4), (0, 4), (4, 4), (4, 4), (8, 4), (8, 4), (12, 2), (14, 2)]
UNIT0 = [0, 8, 16, 24, 32, 40, 48, 52]
UNITS = 56
SPLIT = 24

COLS = {}


def _cols():
    at = 0
    for name, n in (("c", 16), ("norm1", 8), ("norm2", 8), ("convw", 36), ("convb", 12), ("qn", 2), ("kvn", 1),
                    ("modb", 48), ("freq", 1), ("b1", 1), ("b2", 1), ("b3", 1), ("gq", 1), ("gk", 1)):
        COLS[name] = at
        at += n
    return at


NPAR = _cols()


def constants():
    t = np.linspace(0.0, 1.0, T, dtype=np.float32)
    bands = 16
    w_ang = (2.0 * math.pi * np.arange(T, dtype=np.float32) / T).astype(np.float32)
    f = np.linspace(1e-4, bands - 1, bands, dtype=np.float32)
    ang = (f[None, :] * w_ang[:, None]).astype(np.float32)
    z = np.concatenate([t[:, None], np.cos(ang), -np.sin(ang)], axis=1).astype(np.float32)
    back = np.r_[0, np.arange(T - 1, 0, -1)]
    z2 = np.concatenate([z.T, z[back].T], axis=0)
    lo, hi = math.log(1e-2) / 0.3, math.log(1e-2) / 1.5
    deltas = np.abs(np.linspace(lo, hi, HY, dtype=np.float32))
    decay = np.exp(-t[:, None] * deltas[None, :]).astype(np.float32)
    dec = np.stack([decay, decay[back]], axis=1).reshape(TT, P, 2, HY).transpose(1, 0, 2, 3)
    angles, fwd = [], np.zeros((P, UNITS, P), np.float64)
    for a0, step, n, tiles in FACTORS:
        angles.append(a0 + step * np.arange(n))
    theta = np.concatenate(angles)
    unit = 0
    for pair, (_, tiles) in enumerate(PAIR_TILES):
        th = theta[pair * P:(pair + 1) * P]
        for ri in range(2):
            for k in range(tiles):
                n = k * P + np.arange(P)
                a = n[:, None] * th[None, :]
                m = np.cos(a) if ri == 0 else np.sin(a)
                if pair == 7 and ri == 1:
                    m[:, 0] = (-1.0) ** n
                fwd[:, unit, :] = m
                unit += 1
    n = np.arange(T)
    inv = np.zeros((P, 16, T), np.float64)
    for pair in range(8):
        a = theta[pair * P:(pair + 1) * P][:, None] * n[None, :]
        inv[:, 2 * pair] = np.cos(a) * 2 / 2048
        inv[:, 2 * pair + 1] = np.sin(a) * 2 / 2048
    inv[0, 14] = 1.0 / 2048
    inv[0, 15] = (-1.0) ** n / 2048
    row, col = (np.arange(T) // GRID_W).astype(np.float32), (np.arange(T) % GRID_W).astype(np.float32)
    nf = ROPE // 4
    invf = np.power(np.float32(THETA), -np.arange(nf, dtype=np.float32) / nf).astype(np.float32)
    ra = np.stack([row[:, None] * invf, col[:, None] * invf], axis=1).astype(np.float32)
    rope = np.stack([np.cos(ra), np.sin(ra)]).reshape(2, TT, P, 32).transpose(2, 0, 1, 3)
    small = np.zeros((P, 3 * P + NE + NE + 4 * TT), np.float32)
    small[:, 0:P] = np.eye(P)
    small[:, P:2 * P] = np.triu(np.ones((P, P)), 1)
    small[:, 2 * P:3 * P] = 1.0
    small[:, 3 * P:3 * P + NE] = np.arange(NE)
    small[:, 3 * P + NE:3 * P + 2 * NE] = np.arange(NE) * CAP
    ids = (np.arange(TT)[None, :, None] * P + np.arange(P)[:, None, None]) * TOPK + np.arange(TOPK)
    small[:, 3 * P + 2 * NE:] = ids.reshape(P, TT * TOPK)
    c = np.ascontiguousarray
    return {"k_z": c(z2), "k_decay": c(dec), "k_fwd": c(fwd.astype(np.float32)),
            "k_inv": c(inv.astype(np.float32)), "k_rope": c(rope.astype(np.float32)), "k_small": small}


def layout(v):
    c = np.ascontiguousarray
    col = lambda a: np.asarray(a).reshape(-1, P).T
    two = lambda a: np.concatenate([a, a])[:, None]
    par = [col(v["c"]), col(v["c_ctx"]), col(v["norm1_g"]), col(v["norm2_g"]), col(v["hy_conv_w"]),
           col(v["hy_conv_b"]), col(v["mla_q_norm_g"]), col(v["mla_kv_norm_g"]), col(v["mod_b"]),
           two(v["hy_f_freq"][0]), two(v["hy_f_b1"][0]), two(v["hy_f_b2"][0]), two(v["hy_f_b3"][0]),
           v["qk_norm_q_g"][0][:NOPE, None], v["qk_norm_k_g"][0][:NOPE, None]]
    fw = np.zeros((P, 3 * P + HY), np.float32)
    for i, n in enumerate(("hy_f_w1", "hy_f_w2", "hy_f_w3")):
        w = v[n][0]
        r = w.shape[0]
        fw[0:r, i * P:i * P + 64] = w
        fw[r:2 * r, i * P + 64:(i + 1) * P] = w
    fw[0:64, 3 * P:] = v["hy_f_w4"][0][:, :HY]
    fw[64:, 3 * P:] = v["hy_f_w4"][0][:, HY:]
    rows = np.concatenate([v["mod_b"][0, 2 * D:3 * D], v["router_b"][0], v["qk_norm_q_g"][0][NOPE:],
                           v["qk_norm_k_g"][0][NOPE:]])
    return {"x": c(v["x"][0]), "ctx": c(v["ctx"][0]), "mod_w": c(v["mod_w"][0]), "w_in": c(v["w_in"][0]),
            "par": c(np.concatenate(par, axis=1)), "fw": fw, "hy_bias": c(v["hy_bias"]),
            "rows": c(np.broadcast_to(rows, (P, rows.size))),
            "w_uq": c(v["mla_w_uq"][0]), "w_ukv": c(v["mla_w_ukv"][0]), "w_out": c(v["w_out"][0]),
            "router_w": c(v["router_w"][0]), "w_gu": c(v["exp_w_gu"][0]), "w_down": c(v["exp_w_down"][0]),
            "b_gu": c(v["exp_b_gu"][0].reshape(NE * 16, P).T), "b_dn": c(v["exp_b_down"][0].reshape(NE * 8, P).T)}


KB = 1024
RING0 = 16512
SLOT = 16 * KB
WORK0 = RING0 + 4 * SLOT
PERS0 = 229344 - 12 * KB
FRONT_CHUNKS = 26
WIDTHS = (64, 96, 128, 160, 192, 224, 256, 320, 384, 448, 512)
USES = [sum(j % 4 == i for j in range(FRONT_CHUNKS)) for i in range(4)] + [0, 0]
LIMIT = 7.0
ALPHA = 1.702


def build(nc, a, out):
    S = ExitStack()

    def at(name, kb, shape, dt=F32, base=WORK0):
        return nc.alloc_sbuf_tensor_at(name, shape, dt, offset=base + int(kb * KB))

    def dram(name, shape, dt=F32):
        return nc.dram_tensor(name, shape, dt, kind="Internal").ap()

    with S:
        sems = {}

        def sem(name):
            sems[name] = S.enter_context(nc.semaphore(name))
            return sems[name]

        ring = [at(f"ring{i}", 0, [P, 8, 512], base=RING0 + i * SLOT) for i in range(6)]
        SD = at("SD", 0, [P, 16, HY])
        RES = at("RES", 32, [P, 16, HY])
        TMP = at("TMP", 64, [P, 4, HY])
        DEC = at("DEC", 72, [P, TT, 2, HY])
        ZS = at("ZS", 104, [66, T])
        HA = at("HA", 108, [P, T])
        HB = at("HB", 112, [P, T])
        RN = at("RN", 116, [P, T])
        FW = at("FW", 120, [P, 3 * P + HY])
        AB = at("AB", 124, [P, 2, HY])
        ACCN = at("ACCN", 128, [P, HY])
        HT = at("HT", 32, [P, DT, T])
        HTC = at("HTC", 64, [P, DT, CTX])
        XB = [at("XB0", 72, [P, 4, D]), at("XB1", 88, [P, 4, D])]
        JUNK = at("JUNK", 108, [P, D])
        VTOK = at("VTOK", 72, [P, TT, HY])
        X0T = at("X0T", 88, [P, HC, T])
        X1T = at("X1T", 104, [P, HC, T])
        VTMP = [at("VT0", 122, [P, T]), at("VT1", 126, [P, T])]
        LATB = at("LATB", 104, [P, KT, LAT])
        RESV = at("RESV", 32, [P, 16, HY])
        TMPV = at("TMPV", 64, [P, 4, HY])
        PR = at("PR", 122, [P, 4, HY])
        CQT = at("CQT", 0, [P, 2, T])
        CKT = at("CKT", 8, [P, KEYS])
        KRT = at("KRT", 13, [P, KT, ROPE])
        WUQ = at("WUQ", 16, [P, 2, NH * QK])
        WUKV = at("WUKV", 22, [P, NH * 256])
        ROPT = at("ROPT", 26, [P, 2, TT, 32])
        KVT = at("KVT", 28, [P, KT, 256])
        QTK = at("QTK", 38, [P, TT, QK])
        KRH = at("KRH", 44, [P, KT, ROPE])
        KTN = at("KTN", 47, [P, KEYS])
        KTR = at("KTR", 52, [64, KEYS])
        QTN = at("QTN", 57, [P, T])
        QTR = at("QTR", 61, [64, T])
        PB = [at("PB0", 65, [P, KEYS]), at("PB1", 70, [P, KEYS])]
        PT = at("PT", 75, [P, KT, P])
        RT = at("RT", 81, [P, 2, TT, 32])
        QRO = at("QRO", 83, [P, TT, ROPE])
        JE = at("JE", 85, [P, QR])
        YA = at("YA", 104, [P, NH, T])
        G1B = at("G1B", 0, [P, D])
        XIN = [at("XIN0", 4, [P, D]), at("XIN1", 8, [P, D])]
        XNB = [at("XNB0", 12, [P, D]), at("XNB1", 16, [P, D])]
        JF = at("JF", 20, [P, D])
        H2T = [at("H2T0", 24, [P, DT, P]), at("H2T1", 28, [P, DT, P])]
        RW = at("RW", 32, [P, DT, NE])
        SREP = at("SREP", 36, [P, DT, P])
        G1R = at("G1R", 40, [P, D])
        XNEW = at("XNEW", 54, [P, 2, D])
        LF = at("LF", 127, [P, NE * LCOL])
        XSR = at("XSR", 32, [P, NB, D])
        XST = at("XST", 48, [P, DT, BLK])
        HE = at("HE", 64, [P, DT, BLK])
        YT = at("YT", 80, [P, DT, BLK])
        TG = at("TG", 96, [P, 4, BLK])
        GA = at("GA", 104, [P, 2, BLK])
        SG = at("SG", 108, [P, 2, BLK])
        U1 = at("U1", 112, [P, BLK])
        YR = at("YR", 114, [P, NB, D])
        YQ = [at("YQ0", 0, [P, TOPK, D]), at("YQ1", 16, [P, TOPK, D])]
        XR = [at("XR0", 88, [P, D]), at("XR1", 92, [P, D])]
        pers = [0]

        def keep(name, shape, dt=F32):
            n = 4 * int(np.prod(shape[1:]))
            t = nc.alloc_sbuf_tensor_at(name, shape, dt, offset=PERS0 + pers[0])
            pers[0] += (n + 31) // 32 * 32
            assert PERS0 + pers[0] <= 229344, name
            return t

        SM = keep("SM", [P, 3 * P + 2 * NE + 4 * TT])
        ID, TRI, ONE = SM[:, 0:P], SM[:, P:2 * P], SM[:, 2 * P:3 * P]
        IOTA, EBASE = SM[:, 3 * P:3 * P + NE], SM[:, 3 * P + NE:3 * P + 2 * NE]
        PIDS = SM[:, 3 * P + 2 * NE:]
        PAR = keep("PAR", [P, NPAR])
        ROWS = keep("ROWS", [P, NE + 2 * ROPE])
        SIL = keep("SIL", [P, 16])
        MODC = keep("MODC", [P, 5, DT, 2])
        A1 = keep("A1", [P, DT, 2])
        A2 = keep("A2", [P, DT])
        RNC = keep("RNC", [P, HC])
        ST = keep("ST", [P, 128])
        FB = keep("FB", [P, 4])
        BGU = keep("BGU", [P, NE * 16])
        BDN = keep("BDN", [P, NE * 8])
        GATE = keep("GATE", [P, TT, TOPK])
        SLOTI = keep("SLOTI", [P, TT, TOPK], I32)
        CNT = keep("CNT", [P, NE + 1], I32)
        LPAIR = keep("LPAIR", [P, (NE + 1) * LCOL], I32)
        LTOK = keep("LTOK", [P, (NE + 1) * LCOL], I32)
        IXG = keep("IXG", [P, NB], I32)
        IXS = keep("IXS", [P, NB], I32)
        RTW = keep("RTW", [P, 8 * NE + 64])

        ps = S.enter_context(nc.psum_tensor("ps", [P, 8, 512], F32))

        def banks(b, n=2):
            return ps[:, b:b + n, :].rearrange("p b f -> p (b f)")

        xn_d = dram("xn_d", [T, D])
        xnew_d = dram("xnew_d", [T, D])
        list_d = dram("list_d", [NE * CAP, 1])
        y_d = dram("y_d", [PAIRS, D])

        full = [sem(f"slot_full{i}") for i in range(6)]
        free = [sem(f"slot_free{i}") for i in range(6)]
        filt_in, par_in, stage, dve_step, act_step = map(sem, ("filt_in", "par_in", "stage", "dve_step", "act_step"))
        mlp_mm, mlp_arg, mlp_sin, fk_mm, fk_done, norm_mm, norm_ev, kres, ku_mm, kev = map(sem, (
            "mlp_mm", "mlp_arg", "mlp_sin", "fk_mm", "fk_done", "norm_mm", "norm_ev", "kres", "ku_mm", "kev"))
        sil_in, sil_ready, mod_mm, mod_ready = map(sem, ("sil_in", "sil_ready", "mod_mm", "mod_ready"))
        x_in = [sem(f"x_in{g}") for g in range(3)]
        ssq_ready, var_ready, std_ready, xn_ready, tp_mm, tp_act, tp_dve = map(sem, (
            "ssq_ready", "var_ready", "std_ready", "xn_ready", "tp_mm", "tp_act", "tp_dve"))
        cv_mm, cv_act, cv_done, v_ready, vt_mm, vt_ev, lat_mm, lat_ev = map(sem, (
            "cv_mm", "cv_act", "cv_done", "v_ready", "vt_mm", "vt_ev", "lat_mm", "lat_ev"))
        vres, u_mm, y_prod, inv_mm, hy_done = map(sem, ("vres", "u_mm", "y_prod", "inv_mm", "hy_done"))
        att_in, lss, lvar, lstd, ln_ready, lt_mm, lt_ev = map(sem, (
            "att_in", "lss", "lvar", "lstd", "ln_ready", "lt_mm", "lt_ev"))
        q_mm, kv_mm, q_ev, kv_ev, hss, hvar, hstd, h_ready, ht_mm, ht_act, ht_dve = map(sem, (
            "q_mm", "kv_mm", "q_ev", "kv_ev", "hss", "hvar", "hstd", "h_ready", "ht_mm", "ht_act", "ht_dve"))
        s_mm, s_max, p_ready, p_norm, pt_mm, pt_act, pt_dve, o_mm, y_ev = map(sem, (
            "s_mm", "s_max", "p_ready", "p_norm", "pt_mm", "pt_act", "pt_dve", "o_mm", "y_ev"))
        f_in, srep_ready, g1_mm, mod2_mm, mod2_ready, wo_mm, xnew_ready, fss, fvar, fstd, fxn = map(sem, (
            "f_in", "srep_ready", "g1_mm", "mod2_mm", "mod2_ready", "wo_mm", "xnew_ready", "fss", "fvar", "fstd", "fxn"))
        xo_in = [sem(f"xo_in{i}") for i in range(2)]
        xn_out = [sem(f"xn_out{i}") for i in range(2)]
        xnew_out = [sem(f"xnew_out{i}") for i in range(2)]
        xs_in = [sem(f"xs_in{b}") for b in range(NB)]
        y_out = [sem(f"y_out{b}") for b in range(NB)]
        rows_init, gu_done, gu_evac, sg_ready, tg_step, u1_step, he_ready, y_done, yt_ready, tp_done, tp_evac, yr_free, ix_step = map(sem, (
            "rows_init", "gu_done", "gu_evac", "sg_ready", "tg_step", "u1_step", "he_ready", "y_done", "yt_ready", "tp_done", "tp_evac", "yr_free", "ix_step"))
        pool_mark = sem("pool_mark")
        yq_in = [sem(f"yq_in{i}") for i in range(2)]
        o_out = [sem(f"o_out{i}") for i in range(2)]
        sum_step, sum_ready = map(sem, ("sum_step", "sum_ready"))
        ft_mm, ft_act, ft_dve, lg_mm, route_m, rk_mm, gexp, gneg, slot_ready, cnt_mm, cnt_ready = map(sem, (
            "ft_mm", "ft_act", "ft_dve", "lg_mm", "route_m", "rk_mm", "gexp", "gneg", "slot_ready", "cnt_mm", "cnt_ready"))
        list_fill, list_init, list_out, list_in, list_mm, list_ready = map(sem, (
            "list_fill", "list_init", "list_out", "list_in", "list_mm", "list_ready"))

        block = S.enter_context(nc.Block())

        def stage_end(eng, n):
            eng.drain().then_inc(stage, 1)
            eng.wait_ge(stage, 4 * n)

        def by_width(eng, count, widths, body):
            if len(widths) == 1:
                body(widths[0])
                return
            with eng.If(count < widths[0] + 1):
                body(widths[0])
            with eng.Else():
                by_width(eng, count, widths[1:], body)

        def passes(eng, one):
            def load(col):
                return eng.value_load(CNT[0:1, bass.ds(col, 1)], min_val=0, max_val=CAP)

            with eng.Fori(0, NE) as e:
                one(e, e, 0, load(e), load(e + 1))
            most = eng.value_load(CNT[0:1, NE:NE + 1], min_val=0, max_val=CAP)
            with eng.If(most > BLK):
                number = eng.alloc_register("pass_number")
                eng.reg_mov(number, NE)
                with eng.Fori(0, NE) as e:
                    c = load(e)
                    with eng.If(c > BLK):
                        it = eng.snap(number, min_val=NE, max_val=2 * NE)
                        one(it, e, 1, c - BLK, c - BLK)
                        eng.reg_add(number, number, 1)

        @block.sync
        def _(sp):
            mod = a["mod_w"].rearrange("(k p) n -> p k n", p=P)
            win = a["w_in"].rearrange("(k p) n -> p k n", p=P)
            wout = a["w_out"].rearrange("(k p) n -> p k n", p=P)
            fwd = [(0, SPLIT), (SPLIT, UNITS)]
            chunks = [("fwd", n) for n in range(2)] + [("mod", n) for n in (0, 1, 2, 3)] + \
                [("in", n) for n in range(4)] + [("fwd", n) for n in range(2)] + [("inv", n) for n in range(4)] + \
                [("mod", n) for n in (4, 5, 6, 7, 8, 9, 10, 11)] + [("out", n) for n in range(2)]
            assert len(chunks) == FRONT_CHUNKS
            for j, (kind, n) in enumerate(chunks):
                slot = ring[j % 4]
                if j >= 4:
                    sp.wait_ge(free[j % 4], j // 4)
                if kind == "fwd":
                    u0, u1 = fwd[n]
                    dst = slot[:, :, :].rearrange("p a b -> p (a b)")[:, 0:(u1 - u0) * P]
                    src = a["k_fwd"][:, u0:u1, :].rearrange("p u m -> p (u m)")
                elif kind == "inv":
                    dst = slot[:, :, :].rearrange("p a b -> p (a b)")
                    src = a["k_inv"][:, 4 * n:4 * n + 4, :].rearrange("p u m -> p (u m)")
                elif kind == "in" and n == 3:
                    dst, src = slot[:, :, 0:LAT], win[:, :, 3 * HY:INC]
                else:
                    dst, src = slot[:, :, :], {"mod": mod, "in": win, "out": wout}[kind][:, :, n * 512:(n + 1) * 512]
                sp.dma_start(dst, src).then_inc(full[j % 4], 16)
            sp.wait_ge(cnt_ready, 1)

            def weights(it, e, block, count, count_next):
                gu = a["w_gu"][bass.ds(e, 1), :, :].rearrange("o (k p) n -> p (o k) n", p=P)
                dn = a["w_down"][bass.ds(e, 1), :, :].rearrange("o (k p) n -> p (o k) n", p=P)
                for c in range(6):
                    src = gu[:, :, FF * (c % 2) + 512 * (c // 2):][:, :, 0:512] if c < 4 else dn[:, :, 512 * (c - 4):][:, :, 0:512]
                    sp.wait_ge(free[c], it + (USES[c] if c < 4 else 1))
                    sp.dma_start(ring[c][:, :, :], src).then_inc(full[c], 16)

            passes(sp, weights)
            sp.wait_ge(stage, 4 * 7)
            yv = y_d.rearrange("(i p k) d -> i p (k d)", p=P, k=TOPK)
            for i in range(TT):
                if i >= 2:
                    sp.wait_ge(sum_ready, i - 1)
                    sp.wait_ge(o_out[i % 2], 16 * (i // 2))
                sp.dma_start(YQ[i % 2][:, :, :].rearrange("p k d -> p (k d)"), yv[i]).then_inc(yq_in[i % 2], 16)
                sp.dma_start(XR[i % 2][:, :], xnew_d[i * P:(i + 1) * P, :]).then_inc(yq_in[i % 2], 16)

        def arrived(pe, j):
            pe.wait_ge(full[j % 4], 16 * (j // 4 + 1))

        @block.tensor
        def _(pe):
            mm = nc.tensor.matmul
            pe.wait_ge(filt_in, 16 * 3)
            for l in range(3):
                if l:
                    pe.wait_ge(mlp_sin, l)
                for h in range(2):
                    src = (ZS, HA, HB)[l]
                    rows = 66 if l == 0 else P
                    mm(ps[:, h, :], FW[0:rows, l * P:(l + 1) * P], src[0:rows, h * 512:(h + 1) * 512],
                       start=True, stop=True).then_inc(mlp_mm, 1)
            pe.wait_ge(mlp_sin, 3)
            for i in range(TT):
                if i >= 2:
                    pe.wait_ge(fk_done, i - 1)
                b = 2 * (i % 2)
                mm(ps[:, b, :], HA[0:64, i * P:(i + 1) * P], FW[0:64, 3 * P:], start=True, stop=True)
                mm(ps[:, b + 1, :], HA[64:P, i * P:(i + 1) * P], FW[64:P, 3 * P:], start=True, stop=True).then_inc(fk_mm, 1)
            pe.wait_ge(fk_done, TT)
            mm(ps[0:1, 4, :], ONE[:, 0:1], ACCN[:, :], start=True, stop=True)
            for c in range(HC):
                ins = mm(ps[:, 5, c:c + 1], ACCN[:, c * P:(c + 1) * P], ONE[:, 0:1], start=True, stop=True)
            ins.then_inc(norm_mm, 1)

            def transforms(res, first_chunk, ready, ring_wait, done):
                pe.wait_ge(ready, 1)
                for pair, (k0, tiles) in enumerate(PAIR_TILES):
                    if pair == 0:
                        arrived(pe, first_chunk)
                    if UNIT0[pair] == SPLIT:
                        arrived(pe, first_chunk + 1)
                    ring_wait(pair)
                    u = UNIT0[pair]
                    w = ring[(first_chunk + (u >= SPLIT)) % 4][:, :, :].rearrange("p a b -> p (a b)")
                    u -= SPLIT * (u >= SPLIT)
                    for ri in range(2):
                        for k in range(tiles):
                            n = u + ri * tiles + k
                            ins = mm(ps[:, 2 * (pair % 4) + ri, :], w[:, n * P:(n + 1) * P], res[:, k0 + k, :],
                                     start=k == 0, stop=k == tiles - 1)
                    ins.then_inc(done, 1)
                    if pair in (2, 7):
                        pe.wait_ge(done, pair + 1)
                        pe.sem_inc(free[(first_chunk + (pair == 7)) % 4], 1)

            def k_wait(pair):
                if pair >= 4:
                    pe.wait_ge(kev, 2 * (pair - 3))
            transforms(RES, 0, kres, k_wait, ku_mm)
            stage_end(pe, 1)

            pe.wait_ge(sil_ready, 1)

            def mod_columns(chunk, col, bank, done):
                arrived(pe, chunk)
                for m in range(4):
                    for k in range(DT):
                        ins = mm(ps[:, bank, 2 * (col + m):2 * (col + m) + 2], ring[chunk % 4][:, k, m * P:(m + 1) * P],
                                 SIL[:, k:k + 9:8], start=k == 0, stop=k == DT - 1)
                ins.then_inc(done, 1)

            for q in range(4):
                mod_columns(2 + q, 4 * q, 0, mod_mm)
                pe.wait_ge(mod_mm, q + 1)
                pe.sem_inc(free[(2 + q) % 4], 1)
            for g in range(3):
                pe.wait_ge(xn_ready, g + 1)
                width = 4 if g < 2 else CT
                for k in range(DT):
                    n = g * DT + k
                    if n >= 4:
                        pe.wait_ge(tp_act if n % 2 == 0 else tp_dve, (n - 4) // 2 + 1)
                    for j in range(width):
                        ins = nc.tensor.transpose(ps[:, 4 + n % 4, j * P:(j + 1) * P],
                                                  XB[g % 2][:, j, k * P:(k + 1) * P], ID)
                    ins.then_inc(tp_mm, 1)
            stage_end(pe, 2)

            def v_transposes(c):
                pe.wait_ge(v_ready, c + 1)
                for g in range(2):
                    n = 2 * c + g
                    if n >= 4:
                        pe.wait_ge(vt_ev, n - 3)
                    for j in range(4):
                        i = 4 * g + j
                        ins = nc.tensor.transpose(ps[:, 4 + n % 4, j * P:(j + 1) * P], VTMP[c % 2][:, i * P:(i + 1) * P], ID)
                    ins.then_inc(vt_mm, 1)

            for t in range(12):
                chunk = 6 + t // 4
                if t % 4 == 0:
                    arrived(pe, chunk)
                if t >= 2:
                    pe.wait_ge(cv_done, t - 1)
                for h in range(2):
                    for k in range(DT):
                        ins = mm(ps[:, 2 * (t % 2) + h, :], ring[chunk % 4][:, k, (t % 4) * P:(t % 4 + 1) * P],
                                 HT[:, k, h * 512:(h + 1) * 512], start=k == 0, stop=k == DT - 1)
                ins.then_inc(cv_mm, 1)
                if t % 4 == 3:
                    pe.wait_ge(cv_mm, t + 1)
                    pe.sem_inc(free[chunk % 4], 1)
                if t >= 9:
                    v_transposes(t - 9)
            v_transposes(3)
            arrived(pe, 9)
            pe.wait_ge(v_ready, HC)
            for n in range(KT):
                if n < 4:
                    pe.wait_ge(cv_done, 12)
                else:
                    pe.wait_ge(lat_ev, n - 3)
                w, c0 = (HT, 0) if n < TT else (HTC, QR)
                i = n if n < TT else n - TT
                for k in range(DT):
                    ins = mm(ps[:, n % 4, c0:LAT], w[:, k, i * P:(i + 1) * P], ring[9 % 4][:, k, c0:LAT],
                             start=k == 0, stop=k == DT - 1)
                ins.then_inc(lat_mm, 1)
            pe.wait_ge(lat_mm, KT)
            pe.sem_inc(free[9 % 4], 1)
            stage_end(pe, 3)

            def u_wait(pair):
                if pair >= 4:
                    pe.wait_ge(y_prod, pair - 3)
            transforms(RESV, 10, vres, u_wait, u_mm)
            pe.wait_ge(y_prod, 8)
            for j in range(16):
                chunk = 12 + j // 4
                if j % 4 == 0:
                    arrived(pe, chunk)
                w = ring[chunk % 4][:, :, :].rearrange("p a b -> p (a b)")
                for c in range(HC):
                    for h in range(2):
                        ins = mm(ps[:, 2 * c + h, :], SD[:, j, c * P:(c + 1) * P],
                                 w[:, (j % 4) * T + h * 512:(j % 4) * T + (h + 1) * 512], start=j == 0, stop=j == 15)
                        if j == 15 and h == 1:
                            ins.then_inc(inv_mm, 1)
                if j % 4 == 3 and j < 15:
                    ins.then_inc(free[chunk % 4], 1)
            pe.wait_ge(inv_mm, HC)
            pe.sem_inc(free[15 % 4], 1)
            stage_end(pe, 4)

            pe.wait_ge(ln_ready, 1)
            for n in range(7):
                tiles = [range(0, 4), range(4, 8)][n % 2] if n < 4 else [range(0, 4), range(4, 8), range(8, 10)][n - 4]
                c0 = (n // 2) * P if n < 4 else QR
                for j, i in enumerate(tiles):
                    ins = nc.tensor.transpose(ps[:, n, j * P:(j + 1) * P], LATB[:, i, c0:c0 + P], ID)
                ins.then_inc(lt_mm, 1)
            pe.wait_ge(lt_ev, 7)
            pe.wait_ge(att_in, 16 * 3)
            for h in range(NH):
                if h:
                    pe.wait_ge(y_ev, TT * h)
                for b in range(4):
                    for j in range(2):
                        i = 2 * b + j
                        for k in range(2):
                            ins = mm(ps[:, b, j * QK:(j + 1) * QK], CQT[:, k, i * P:(i + 1) * P],
                                     WUQ[:, k, h * QK:(h + 1) * QK], start=k == 0, stop=k == 1)
                    ins.then_inc(q_mm, 1)
                for b in range(5):
                    if b == 4:
                        pe.wait_ge(q_ev, 4 * h + 1)
                    for j in range(2):
                        i = 2 * b + j
                        ins = mm(ps[:, (4 + b) % 8, j * 256:(j + 1) * 256], CKT[:, i * P:(i + 1) * P],
                                 WUKV[:, h * 256:(h + 1) * 256], start=True, stop=True)
                    ins.then_inc(kv_mm, 1)
                pe.wait_ge(h_ready, h + 1)
                for g in range(10):
                    if g < 2:
                        src = [(QTK[:, i, 0:NOPE], P) for i in range(4 * g, 4 * g + 4)]
                    elif g < 4:
                        src = [(QRO[:, i, :], ROPE) for i in range(4 * g - 8, 4 * g - 4)]
                    elif g < 7:
                        src = [(KVT[:, i, 0:NOPE], P) for i in range(4 * g - 16, min(4 * g - 12, KT))]
                    else:
                        src = [(KRH[:, i, :], ROPE) for i in range(4 * g - 28, min(4 * g - 24, KT))]
                    if g >= 8:
                        pe.wait_ge(ht_act, 5 * h + g - 7)
                    for j, (t, rows) in enumerate(src):
                        ins = nc.tensor.transpose(ps[0:rows, g % 8, j * P:(j + 1) * P], t, ID)
                    ins.then_inc(ht_mm, 1)
                pe.wait_ge(ht_act, 5 * h + 5)
                pe.wait_ge(ht_dve, 5 * h + 5)

                def scores(i):
                    u = TT * h + i
                    for seg, (k0, k1) in enumerate(((0, 512), (512, 1024), (1024, KEYS))):
                        o = ps[:, 3 * (u % 2) + seg, 0:k1 - k0]
                        mm(o, QTN[:, i * P:(i + 1) * P], KTN[:, k0:k1], start=True, stop=False)
                        ins = mm(o, QTR[:, i * P:(i + 1) * P], KTR[:, k0:k1], start=False, stop=True)
                    ins.then_inc(s_mm, 1)

                def values(i):
                    u = TT * h + i
                    pe.wait_ge(p_norm, u + 1)
                    for g in range(3):
                        if g == 0 and u:
                            pe.wait_ge(pt_act, 2 * u)
                        if g == 1 and u:
                            pe.wait_ge(y_ev, u)
                        if g == 2:
                            pe.wait_ge(pt_act, 2 * u + 1)
                        for j in range(4 if g < 2 else 2):
                            kt = 4 * g + j
                            ins = nc.tensor.transpose(ps[:, 6 + g % 2, j * P:(j + 1) * P], PB[u % 2][:, kt * P:(kt + 1) * P], ID)
                        ins.then_inc(pt_mm, 1)
                    pe.wait_ge(pt_dve, u + 1)
                    for kt in range(KT):
                        if kt == 8:
                            pe.wait_ge(pt_act, 2 * u + 2)
                        ins = mm(ps[:, 7, 0:P], KVT[:, kt, NOPE:], PT[:, kt, :], start=kt == 0, stop=kt == KT - 1)
                    ins.then_inc(o_mm, 1)

                for i in range(TT + 1):
                    if i < TT:
                        scores(i)
                    if i:
                        values(i - 1)
            stage_end(pe, 5)

            pe.wait_ge(srep_ready, 1)
            for q in range(2):
                arrived(pe, 16 + q)
                for k in range(DT):
                    ins = mm(ps[:, q, :], SREP[:, k, :], ring[(16 + q) % 4][:, k, :], start=k == 0, stop=k == DT - 1)
                ins.then_inc(g1_mm, 1)
                pe.wait_ge(g1_mm, q + 1)
                pe.sem_inc(free[(16 + q) % 4], 1)
            for q in range(6):
                mod_columns(18 + q, 4 * q, 2, mod2_mm)
                pe.wait_ge(mod2_mm, q + 1)
                pe.sem_inc(free[(18 + q) % 4], 1)
            arrived(pe, 24)
            arrived(pe, 25)
            pe.wait_ge(f_in, 32)

            def project(i):
                for h in range(2):
                    if i < 2 and h == 0:
                        pe.wait_ge(mod2_ready, 1)
                    if i >= 2 and h == 0:
                        pe.wait_ge(xnew_ready, i - 1)
                    for k in range(DT):
                        lhs = X0T[:, k, i * P:(i + 1) * P] if k < HC else YA[:, k - HC, i * P:(i + 1) * P]
                        ins = mm(ps[:, 2 * (i % 2) + h, :], lhs, ring[(24 + h) % 4][:, k, :], start=k == 0, stop=k == DT - 1)
                ins.then_inc(wo_mm, 1)

            def route(i):
                pe.wait_ge(fxn, i + 1)
                for g in range(2):
                    n = 2 * i + g
                    if n >= 2:
                        pe.wait_ge(ft_act if g == 0 else ft_dve, i)
                    for j in range(4):
                        k = 4 * g + j
                        ins = nc.tensor.transpose(ps[:, 4 + g, j * P:(j + 1) * P], XNB[i % 2][:, k * P:(k + 1) * P], ID)
                    ins.then_inc(ft_mm, 1)
                pe.wait_ge(ft_act, i + 1)
                pe.wait_ge(ft_dve, i + 1)
                for k in range(DT):
                    ins = mm(ps[:, 6, 0:NE], H2T[i % 2][:, k, :], RW[:, k, :], start=k == 0, stop=k == DT - 1)
                ins.then_inc(lg_mm, 1)
                pe.wait_ge(route_m, i + 1)
                mm(ps[:, 7, 0:NE], TRI, RTW[:, NE:2 * NE], start=True, stop=False)
                mm(ps[:, 7, 0:NE], ONE, RTW[:, 2 * NE:3 * NE], start=False, stop=True).then_inc(rk_mm, 1)

            for i in range(TT + 1):
                if i < TT:
                    project(i)
                if i:
                    route(i - 1)
            pe.wait_ge(slot_ready, TT)
            mm(ps[:, 7, 0:NE], ONE, RTW[:, 2 * NE:3 * NE], start=True, stop=True).then_inc(cnt_mm, 1)
            pe.wait_ge(list_in, 32)
            for g in range(2):
                ins = nc.tensor.transpose(ps[:, 6, g * P:(g + 1) * P], JF[:, g * P:(g + 1) * P], ID)
            ins.then_inc(list_mm, 1)
            stage_end(pe, 6)

            pe.wait_ge(cnt_ready, 1)
            for c in (0, 1, 4, 5):
                pe.sem_inc(free[c], 1)
            def turn_rows(g, base, count):
                for b in range(NB):
                    pe.wait_ge(xs_in[b], g * 16 + 16)

                def body(w):
                    for k in range(DT):
                        pe.wait_ge(tp_evac, base + k + 1)
                        for b in range(w // P):
                            ins = nc.tensor.transpose(ps[:, 6 + k % 2, b * P:(b + 1) * P], XSR[:, b, k * P:(k + 1) * P], ID)
                        ins.then_inc(tp_done, 1)
                by_width(pe, count, (128, 256, 384, 512), body)

            def one(it, e, block, count, count_next):
                if block:
                    turn_rows(it + 1, it * 16 + 8, count)
                    pe.wait_ge(tp_evac, it * 16 + 18)
                else:
                    pe.wait_ge(tp_evac, it * 16 + 2)

                def gate_up(w):
                    for c in range(4):
                        pe.wait_ge(full[c], (it + 1 + USES[c]) * 16)
                        for m in range(4):
                            t = 4 * c + m
                            pe.wait_ge(gu_evac, it * 16 + t + 1)
                            for k in range(DT):
                                ins = mm(ps[:, m, 0:w], ring[c][:, k, m * P:(m + 1) * P], XST[:, k, 0:w],
                                         start=k == 0, stop=k == DT - 1)
                                if m == 0 and k == 0 and c:
                                    ins.then_inc(free[c - 1], 1)
                            ins.then_inc(gu_done, 1)
                by_width(pe, count, WIDTHS, gate_up)
                if not block:
                    turn_rows(it + 1, it * 16 + 8, count_next)

                def down(w):
                    for c in range(2):
                        pe.wait_ge(full[4 + c], (it + 1) * 16)
                        for m in range(4):
                            d = 4 * c + m
                            pe.wait_ge(yt_ready, it * 8 + d + 1)
                            for k in range(DT):
                                if d == 0:
                                    pe.wait_ge(he_ready, it * 8 + k + 1)
                                ins = mm(ps[:, 4 + d % 2, 0:w], ring[4 + c][:, k, m * P:(m + 1) * P], HE[:, k, 0:w],
                                         start=k == 0, stop=k == DT - 1)
                                if m == 0 and k == 0:
                                    ins.then_inc(free[3 + c], 1)
                            ins.then_inc(y_done, 1)
                    nb = (w + P - 1) // P
                    for g in range(2 * nb):
                        pe.wait_ge(tp_evac, it * 16 + 16 + g + 1)
                        for j in range(4):
                            k = 4 * (g % 2) + j
                            if g < 2:
                                pe.wait_ge(yt_ready, it * 8 + k + 3)
                            ins = nc.tensor.transpose(ps[:, 6 + g % 2, j * P:(j + 1) * P],
                                                      YT[:, k, (g // 2) * P:(g // 2 + 1) * P], ID)
                            if g == 0 and j == 0:
                                ins.then_inc(free[5], 1)
                        ins.then_inc(tp_done, 1 if g < 2 * nb - 1 else 1 + 2 * (NB - nb))
                by_width(pe, count, WIDTHS, down)

            turn_rows(0, 0, pe.value_load(CNT[0:1, 0:1], min_val=0, max_val=CAP))
            pe.wait_ge(tp_evac, 10)
            passes(pe, one)
            stage_end(pe, 7)

        @block.scalar
        def _(act):
            n_step = [0]

            def step(ins):
                n_step[0] += 1
                ins.then_inc(act_step, 1)
                act.wait_ge(act_step, n_step[0])

            made = {}

            def give(ins, ready):
                made[ready] = made.get(ready, 0) + 1
                ins.then_inc(ready, 1)
                act.wait_ge(ready, made[ready])

            fn = nc.scalar.activation
            act.dma_start(ZS[:, :], a["k_z"]).then_inc(filt_in, 16)
            act.dma_start(FW[:, :], a["fw"]).then_inc(filt_in, 16)
            act.dma_start(SM[:, :], a["k_small"]).then_inc(filt_in, 16)
            act.dma_start(PAR[:, :], a["par"]).then_inc(par_in, 16)
            act.dma_start(DEC[:, :, :, :].rearrange("p t r c -> p (t r c)"),
                          a["k_decay"].rearrange("p t r c -> p (t r c)")).then_inc(par_in, 16)
            act.dma_start(ACCN[0:1, :], a["hy_bias"]).then_inc(par_in, 16)
            act.dma_start(BGU[:, :], a["b_gu"]).then_inc(par_in, 16)
            act.dma_start(BDN[:, :], a["b_dn"]).then_inc(par_in, 16)
            act.dma_start(ROWS[:, :], a["rows"][:, D:]).then_inc(par_in, 16)
            for l in range(3):
                act.wait_ge(mlp_arg, l + 1)
                give(fn((HA, HB, HA)[l][:, :], (HB, HA, HB)[l][:, :], ACT.Sin), mlp_sin)
            for pair in range(8):
                act.wait_ge(ku_mm, pair + 1)
                for ri in range(2):
                    if pair == 0 and ri == 0:
                        act.wait_ge(kres, 1)
                    give(fn(SD[:, 2 * pair + ri, :], ps[:, 2 * (pair % 4) + ri, :], ACT.Copy), kev)
            give(fn(SIL[:, :], PAR[:, COLS["c"]:COLS["c"] + 16], ACT.Sigmoid), sil_in)
            stage_end(act, 1)
            x_v = a["x"].rearrange("(i p) d -> p i d", p=P)
            c_v = a["ctx"].rearrange("(i p) d -> p i d", p=P)
            for g in range(2):
                act.dma_start(XB[g][:, :, :], x_v[:, 4 * g:4 * g + 4, :]).then_inc(x_in[g], 16)

            def squares(g):
                act.wait_ge(x_in[g], 16)
                for j in range(4 if g < 2 else CT):
                    n = 4 * g + j
                    step(fn(JUNK[:, :], XB[g % 2][:, j, :], ACT.Square, accum_out=ST[:, n:n + 1]))
                act.nop().then_inc(ssq_ready, 1)

            def root(ready, lo, hi, done, n):
                act.wait_ge(ready, n)
                give(fn(ST[:, lo:hi], ST[:, lo:hi], ACT.Sqrt), done)

            def fill(g):
                for k in range(0, DT, 2):
                    act.wait_ge(tp_mm, g * DT + k + 1)
                    dst, s = (HT[:, k, g * 512:(g + 1) * 512], 0) if g < 2 else (HTC[:, k, :], 1)
                    w = 512 if g < 2 else CTX
                    give(fn(dst, ps[:, 4 + (g * DT + k) % 4, 0:w], ACT.Identity, scale=A1[:, k, s:s + 1],
                       bias=MODC[:, 0, k, s:s + 1]), tp_act)

            squares(0)
            root(var_ready, 10, 14, std_ready, 1)
            squares(1)
            root(var_ready, 14, 18, std_ready, 2)
            act.wait_ge(mod_ready, 1)
            fill(0)
            act.wait_ge(tp_mm, DT)
            act.dma_start(XB[0][:, 0:CT, :], c_v).then_inc(x_in[2], 16)
            squares(2)
            root(var_ready, 18, 20, std_ready, 3)
            fill(1)
            fill(2)
            stage_end(act, 2)
            for t in range(12):
                dst = X0T[:, t, :] if t < 4 else X1T[:, t - 4, :] if t < 8 else VTMP[t % 2][:, :]
                if t >= 10:
                    act.wait_ge(vt_mm, 2 * (t - 9))
                act.wait_ge(cv_mm, t + 1)
                w1 = COLS["convw"] + 12 + t
                give(fn(dst, banks(2 * (t % 2)), ACT.Identity, scale=PAR[:, w1:w1 + 1],
                   bias=PAR[:, COLS["convb"] + t:COLS["convb"] + t + 1]), cv_act)
                if t in (10, 11):
                    for g in range(2):
                        n = 2 * (t - 10) + g
                        act.wait_ge(vt_mm, n + 1)
                        give(fn(VTOK[:, 4 * g:4 * g + 4, (t - 10) * P:(t - 9) * P],
                           ps[:, 4 + n % 4, :].rearrange("p (i c) -> p i c", c=P), ACT.Copy), vt_ev)
            for n in range(4, 8):
                act.wait_ge(vt_mm, n + 1)
                give(fn(VTOK[:, 4 * (n % 2):4 * (n % 2) + 4, (n // 2) * P:(n // 2 + 1) * P],
                   ps[:, 4 + n % 4, :].rearrange("p (i c) -> p i c", c=P), ACT.Copy), vt_ev)
            for n in range(KT):
                act.wait_ge(lat_mm, n + 1)
                c0 = 0 if n < TT else QR
                give(fn(LATB[:, n, c0:LAT], ps[:, n % 4, c0:LAT], ACT.Copy), lat_ev)
            stage_end(act, 3)
            stage_end(act, 4)
            act.dma_start(WUQ[:, :, :], a["w_uq"].rearrange("(k p) n -> p k n", p=P)).then_inc(att_in, 16)
            act.dma_start(WUKV[:, :], a["w_ukv"]).then_inc(att_in, 16)
            act.dma_start(ROPT[:, :, :, :].rearrange("p s t f -> p (s t f)"),
                          a["k_rope"].rearrange("p s t f -> p (s t f)")).then_inc(att_in, 16)
            for n in range(KT):
                if n < TT:
                    step(fn(JE[:, 0:QR], LATB[:, n, 0:QR], ACT.Square, accum_out=ST[:, 20 + n:21 + n]))
                step(fn(JE[:, 0:KR], LATB[:, n, QR:QR + KR], ACT.Square, accum_out=ST[:, 28 + n:29 + n]))
                step(fn(JE[:, 0:ROPE], LATB[:, n, QR + KR:], ACT.Square, accum_out=ST[:, 38 + n:39 + n]))
            act.nop().then_inc(lss, 1)
            root(lvar, 48, 66, lstd, 1)
            for n in range(7):
                act.wait_ge(lt_mm, n + 1)
                if n < 4:
                    c = COLS["qn"] + n // 2
                    give(fn(CQT[:, n // 2, (n % 2) * 512:(n % 2 + 1) * 512], ps[:, n, :], ACT.Copy,
                       scale=PAR[:, c:c + 1]), lt_ev)
                else:
                    g = n - 4
                    w = 512 if g < 2 else 256
                    give(fn(CKT[:, g * 512:g * 512 + w], ps[:, n, 0:w], ACT.Copy,
                       scale=PAR[:, COLS["kvn"]:COLS["kvn"] + 1]), lt_ev)
            for h in range(NH):
                for b in range(4):
                    act.wait_ge(q_mm, 4 * h + b + 1)
                    give(fn(QTK[:, 2 * b:2 * b + 2, :].rearrange("p t c -> p (t c)"), ps[:, b, 0:2 * QK],
                       ACT.Copy), q_ev)
                act.wait_ge(q_ev, 4 * h + 4)
                for i in range(TT):
                    step(fn(JE[:, 0:QK], QTK[:, i, :], ACT.Square, accum_out=ST[:, 66 + i:67 + i]))
                act.wait_ge(kv_ev, 5 * h + 5)
                for i in range(KT):
                    step(fn(JE[:, 0:NOPE], KVT[:, i, 0:NOPE], ACT.Square, accum_out=ST[:, 74 + i:75 + i]))
                act.nop().then_inc(hss, 1)
                root(hvar, 84, 102, hstd, h + 1)
                for g in (0, 1, 4, 5, 6):
                    act.wait_ge(ht_mm, 10 * h + g + 1)
                    if g < 2:
                        give(fn(QTN[:, g * 512:(g + 1) * 512], ps[:, g, :], ACT.Copy, scale=FB[:, 3:4]), ht_act)
                    else:
                        w = 512 if g < 6 else 256
                        give(fn(KTN[:, (g - 4) * 512:(g - 4) * 512 + w], ps[:, g, 0:w], ACT.Copy), ht_act)

                def softmax(i):
                    u = TT * h + i
                    act.wait_ge(s_max, u + 1)
                    if u >= 2:
                        act.wait_ge(pt_mm, 3 * (u - 1))
                    b = 3 * (u % 2)
                    give(fn(PB[u % 2][:, :], banks(b, 3)[:, 0:KEYS], ACT.Exp, bias=ST[:, 104 + u % 2:105 + u % 2],
                       accum_out=ST[:, 106 + u % 2:107 + u % 2]), p_ready)

                def pt_store(i, g):
                    u = TT * h + i
                    act.wait_ge(pt_mm, 3 * u + g + 1)
                    w = 4 if g < 2 else 2
                    give(fn(PT[:, 4 * g:4 * g + w, :].rearrange("p a b -> p (a b)"), ps[:, 6, 0:w * P],
                       ACT.Copy), pt_act)

                for i in range(TT + 1):
                    if i < TT:
                        softmax(i)
                    if i:
                        pt_store(i - 1, 0)
                        pt_store(i - 1, 2)
                        act.wait_ge(o_mm, TT * h + i)
                        give(fn(YA[:, h, (i - 1) * P:i * P], ps[:, 7, 0:P], ACT.Copy), y_ev)
            stage_end(act, 5)
            act.dma_start(RW[:, :, :], a["router_w"].rearrange("(k p) e -> p k e", p=P)).then_inc(f_in, 16)
            act.dma_start(G1R[:, :], a["rows"][:, 0:D]).then_inc(f_in, 16)
            for i in range(2):
                act.dma_start(XIN[i][:, :], a["x"][i * P:(i + 1) * P, :]).then_inc(xo_in[i], 16)
            for i in range(TT + 1):
                if i < TT:
                    act.wait_ge(xnew_ready, i + 1)
                    step(fn(JF[:, :], XNEW[:, i % 2, :], ACT.Square, accum_out=ST[:, i:i + 1]))
                    act.nop().then_inc(fss, 1)
                    if i + 2 < TT:
                        act.dma_start(XIN[i % 2][:, :], a["x"][(i + 2) * P:(i + 3) * P, :]).then_inc(xo_in[i % 2], 16)
                    root(fvar, 10 + i, 11 + i, fstd, i + 1)
                if i:
                    t = i - 1
                    act.wait_ge(ft_mm, 2 * t + 1)
                    act.dma_start(xn_d[t * P:(t + 1) * P, :], XNB[t % 2][:, :]).then_inc(xn_out[t % 2], 16)
                    act.dma_start(xnew_d[t * P:(t + 1) * P, :], XNEW[:, t % 2, :]).then_inc(xnew_out[t % 2], 16)
                    for j in range(4):
                        ins = fn(H2T[t % 2][:, j, :], ps[:, 4, j * P:(j + 1) * P], ACT.Identity, scale=A2[:, j:j + 1],
                                 bias=MODC[:, 2, j, 0:1])
                    give(ins, ft_act)
                    act.wait_ge(gneg, t + 1)
                    give(fn(RTW[:, 8 * NE + 16:8 * NE + 20], RTW[:, 8 * NE:8 * NE + 4], ACT.Exp, bias=RTW[:, 8 * NE + 24:8 * NE + 25],
                            accum_out=RTW[:, 8 * NE + 25:8 * NE + 26]), gexp)
            for i in range(2):
                act.wait_ge(xn_out[i], 16 * (TT // 2))
                act.wait_ge(xnew_out[i], 16 * (TT // 2))
            stage_end(act, 6)

            act.wait_ge(cnt_ready, 1)
            act.sem_inc(tp_evac, 2)

            def store_rows(base, count):
                def body(w):
                    for k in range(DT):
                        act.wait_ge(tp_done, base + k + 1)
                        fn(XST[:, k, 0:w], ps[:, 6 + k % 2, 0:w], ACT.Identity, scale=A2[:, k:k + 1],
                           bias=MODC[:, 2, k, 0:1]).then_inc(tp_evac, 1)
                by_width(act, count, (128, 256, 384, 512), body)

            def one(it, e, block, count, count_next):
                if block:
                    store_rows(it * 16 + 8, count)

                def sigmoids(w):
                    for m in range(DT):
                        act.wait_ge(gu_evac, it * 16 + 4 + 8 * (m // 4) + m % 4 + 1)
                        fn(SG[:, m % 2, 0:w], GA[:, m % 2, 0:w], ACT.Sigmoid, scale=ALPHA).then_inc(sg_ready, 1)
                by_width(act, count, (128, 256, 384, 512), sigmoids)
                if not block:
                    store_rows(it * 16 + 8, count_next)

                def results(w):
                    act.wait_ge(yr_free, it + 1)
                    nb = w // P
                    for g in range(2 * nb):
                        act.wait_ge(tp_done, it * 16 + 16 + g + 1)
                        fn(YR[:, g // 2, (g % 2) * 512:(g % 2 + 1) * 512], ps[:, 6 + g % 2, :],
                           ACT.Copy).then_inc(tp_evac, 1 if g < 2 * nb - 1 else 1 + 2 * (NB - nb))
                by_width(act, count, (128, 256, 384, 512), results)

            store_rows(0, act.value_load(CNT[0:1, 0:1], min_val=0, max_val=CAP))
            passes(act, one)
            stage_end(act, 7)
            for i in range(TT):
                act.wait_ge(sum_ready, i + 1)
                act.dma_start(out[i * P:(i + 1) * P, :], XR[i % 2][:, :]).then_inc(o_out[i % 2], 16)
            for i in range(2):
                act.wait_ge(o_out[i], 16 * (TT // 2))

        @block.vector
        def _(dve):
            n_step = [0]
            v = nc.vector

            def step(ins):
                n_step[0] += 1
                ins.then_inc(dve_step, 1)
                dve.wait_ge(dve_step, n_step[0])

            made = {}

            def give(ins, ready):
                made[ready] = made.get(ready, 0) + 1
                ins.then_inc(ready, 1)
                dve.wait_ge(ready, made[ready])

            tt, ts, stt = v.tensor_tensor, v.tensor_scalar, v.scalar_tensor_tensor
            dve.wait_ge(par_in, 16 * 6)
            fc = PAR[:, COLS["freq"]:COLS["freq"] + 1]
            for l in range(3):
                b = COLS["b1"] + l
                step(tt(FB[:, l:l + 1], PAR[:, b:b + 1], fc, ALU.mult))
            step(tt(FB[:, 3:4], PAR[:, COLS["gq"]:COLS["gq"] + 1], PAR[:, COLS["gk"]:COLS["gk"] + 1], ALU.mult))
            step(ts(FB[:, 3:4], FB[:, 3:4], SCALE, None, ALU.mult))
            c1 = 6.28125
            c2 = 2.0 ** -24 * round((2 * math.pi - c1) * 2.0 ** 24 / 4096) * 4096
            c3 = 2 * math.pi - c1 - c2
            for l in range(3):
                dst = (HB, HA, HB)[l]
                dve.wait_ge(mlp_mm, 2 * l + 2)
                step(ts(dst[:, :], banks(0), fc, FB[:, l:l + 1], ALU.mult, ALU.add))
                step(ts(RN[:, :], dst[:, :], 1 / (2 * math.pi), MAGIC, ALU.mult, ALU.add))
                step(ts(RN[:, :], RN[:, :], MAGIC, None, ALU.subtract))
                for c in (c1, c2, c3):
                    step(stt(out=dst[:, :], in0=RN[:, :], scalar=-c, in1=dst[:, :], op0=ALU.mult, op1=ALU.add))
                give(ts(dst[:, :], dst[:, :], 3.1415925, -3.1415925, ALU.min, ALU.max), mlp_arg)
            step(v.tensor_copy(RN[0:1, 0:HY], ACCN[0:1, :]))
            step(v.memset(ACCN[:, :], 0.0))
            for i in range(TT):
                dve.wait_ge(fk_mm, i + 1)
                b = 2 * (i % 2)
                step(tt(AB[:, :, :].rearrange("p r c -> p (r c)"), banks(b), DEC[:, i, :, :].rearrange("p r c -> p (r c)"), ALU.mult))
                step(stt(out=TMP[:, 0:2, :], in0=AB[:, :, :], scalar=-1.0, in1=AB[:, :, :], op0=ALU.mult, op1=ALU.max))
                for r in range(2):
                    step(tt(ACCN[:, :], ACCN[:, :], TMP[:, r, :], ALU.add))
                if i == 0:
                    step(v.memset(AB[0:1, 1, :], 0.0))
                tt(SD[:, i, :], AB[:, 0, :], AB[:, 1, :], ALU.add)
                give(tt(SD[:, 8 + i, :], AB[:, 0, :], AB[:, 1, :], ALU.subtract), fk_done)
            dve.wait_ge(fk_done, TT)
            dve.wait_ge(norm_mm, 1)
            step(tt(RN[0:1, 0:HY], RN[0:1, 0:HY], ps[0:1, 4, :], ALU.mult))
            v.reciprocal(RNC[:, :], ps[:, 5, 0:HC])
            step(tt(SD[0:1, 0, :], SD[0:1, 0, :], RN[0:1, 0:HY], ALU.add))
            step(tt(SD[0:1, 8, :], SD[0:1, 8, :], RN[0:1, 0:HY], ALU.add))

            def residues(cyc, neg, res, tmp, done):
                s2 = math.sqrt(2.0)
                step(tt(tmp[:, :, :], cyc[:, 0:4, :], cyc[:, 4:8, :], ALU.add))
                step(tt(res[:, 8:12, :], cyc[:, 0:4, :], cyc[:, 4:8, :], ALU.subtract))
                step(tt(res[:, 12:14, :], tmp[:, 0:2, :], tmp[:, 2:4, :], ALU.subtract))
                step(tt(res[:, 14:16, :], tmp[:, 0:2, :], tmp[:, 2:4, :], ALU.add))
                step(tt(tmp[:, 0:2, :], neg[:, 0:2, :], neg[:, 4:6, :], ALU.subtract))
                step(tt(tmp[:, 2:4, :], neg[:, 2:4, :], neg[:, 6:8, :], ALU.add))
                for r, s in ((0, s2), (4, -s2)):
                    step(stt(out=res[:, r:r + 2, :], in0=neg[:, 6:8, :], scalar=s, in1=tmp[:, 0:2, :], op0=ALU.mult, op1=ALU.add))
                    ins = stt(out=res[:, r + 2:r + 4, :], in0=neg[:, 4:6, :], scalar=-s, in1=tmp[:, 2:4, :], op0=ALU.mult, op1=ALU.add)
                    if r == 0:
                        step(ins)
                give(ins, done)

            residues(SD[:, 0:8, :], SD[:, 8:16, :], RES, TMP, kres)
            dve.wait_ge(sil_in, 1)
            give(tt(SIL[:, :], SIL[:, :], PAR[:, COLS["c"]:COLS["c"] + 16], ALU.mult), sil_ready)
            stage_end(dve, 1)

            def inverse_std(lo, n, scale, ready, std, k, off):
                give(ts(ST[:, lo + off:lo + off + n], ST[:, lo:lo + n], scale, EPS, ALU.mult, ALU.add), ready)
                dve.wait_ge(std, k)
                step(v.reciprocal(ST[:, lo + off:lo + off + n], ST[:, lo + off:lo + off + n]))

            def scale_x(g):
                n = 4 if g < 2 else CT
                dve.wait_ge(ssq_ready, g + 1)
                inverse_std(4 * g, n, 1.0 / D, var_ready, std_ready, g + 1, 10)
                for j in range(n):
                    ins = ts(XB[g % 2][:, j, :], XB[g % 2][:, j, :], ST[:, 10 + 4 * g + j:11 + 4 * g + j], None, ALU.mult)
                give(ins, xn_ready)

            def fill(g):
                for k in range(1, DT, 2):
                    dve.wait_ge(tp_mm, g * DT + k + 1)
                    dst, s = (HT[:, k, g * 512:(g + 1) * 512], 0) if g < 2 else (HTC[:, k, :], 1)
                    w = 512 if g < 2 else CTX
                    give(ts(dst, ps[:, 4 + (g * DT + k) % 4, 0:w], A1[:, k, s:s + 1], MODC[:, 0, k, s:s + 1],
                       ALU.mult, ALU.add), tp_dve)

            scale_x(0)
            scale_x(1)
            dve.wait_ge(mod_mm, 4)
            mb = COLS["modb"]
            for s in range(2):
                src = ps[:, 0, 0:32].rearrange("p (m k s) -> p m k s", m=2, s=2)
                step(tt(MODC[:, 0:2, :, s], src[:, :, :, s], PAR[:, mb:mb + 16].rearrange("p (m k) -> p m k", m=2), ALU.add))
                ins = stt(out=A1[:, :, s], in0=MODC[:, 1, :, s], scalar=1.0, in1=PAR[:, COLS["norm1"]:COLS["norm1"] + 8],
                          op0=ALU.add, op1=ALU.mult)
                if s == 0:
                    step(ins)
            give(ins, mod_ready)
            dve.wait_ge(mod_ready, 1)
            fill(0)
            scale_x(2)
            fill(1)
            fill(2)
            stage_end(dve, 2)

            for t in range(12):
                dst = X0T[:, t, :] if t < 4 else X1T[:, t - 4, :] if t < 8 else VTMP[t % 2][:, :]
                dve.wait_ge(cv_act, t + 1)
                w = COLS["convw"] + t
                u = banks(2 * (t % 2))
                step(stt(out=dst[:, 1:T], in0=u[:, 0:T - 1], scalar=PAR[:, w:w + 1], in1=dst[:, 1:T], op0=ALU.mult, op1=ALU.add))
                give(stt(out=dst[:, 0:T - 1], in0=u[:, 1:T], scalar=PAR[:, w + 24:w + 25], in1=dst[:, 0:T - 1],
                    op0=ALU.mult, op1=ALU.add), cv_done)
                if t < 4 or t >= 8:
                    dve.wait_ge(cv_done, t + 1)
                if t < 4:
                    ts(dst, dst, RNC[:, t:t + 1], None, ALU.mult)
                if t >= 8:
                    give(tt(dst, dst, X1T[:, t - 8, :], ALU.mult), v_ready)
            stage_end(dve, 3)

            residues(VTOK[:, :, :], VTOK[:, :, :], RESV, TMPV, vres)
            for pair in range(8):
                dve.wait_ge(u_mm, pair + 1)
                b = 2 * (pair % 4)
                kr, ki = SD[:, 2 * pair, :], SD[:, 2 * pair + 1, :]
                tt(PR[:, 0, :], ps[:, b, :], kr, ALU.mult)
                tt(PR[:, 1, :], ps[:, b + 1, :], ki, ALU.mult)
                tt(PR[:, 2, :], ps[:, b, :], ki, ALU.mult)
                step(tt(PR[:, 3, :], ps[:, b + 1, :], kr, ALU.mult))
                tt(kr, PR[:, 0, :], PR[:, 1, :], ALU.subtract)
                ins = tt(ki, PR[:, 2, :], PR[:, 3, :], ALU.add)
                if pair == 7:
                    step(ins)
                    v.tensor_copy(kr[0:1, :], PR[0:1, 0, :])
                    ins = v.tensor_copy(ki[0:1, :], PR[0:1, 1, :])
                give(ins, y_prod)
                dve.wait_ge(y_prod, pair + 1)
            for c in range(HC):
                dve.wait_ge(inv_mm, c + 1)
                tt(X0T[:, c, :], X0T[:, c, :], banks(2 * c), ALU.mult)
            stage_end(dve, 4)

            dve.wait_ge(lss, 1)
            ts(ST[:, 48:56], ST[:, 20:28], 1.0 / QR, EPS, ALU.mult, ALU.add)
            give(ts(ST[:, 56:66], ST[:, 28:38], 1.0 / KR, EPS, ALU.mult, ALU.add), lvar)
            dve.wait_ge(lstd, 1)
            step(v.reciprocal(ST[:, 48:66], ST[:, 48:66]))
            for n in range(KT):
                if n < TT:
                    ts(LATB[:, n, 0:QR], LATB[:, n, 0:QR], ST[:, 48 + n:49 + n], None, ALU.mult)
                ins = ts(LATB[:, n, QR:QR + KR], LATB[:, n, QR:QR + KR], ST[:, 56 + n:57 + n], None, ALU.mult)
            give(ins, ln_ready)
            for n in range(KT):
                ins = tt(KRT[:, n, :], LATB[:, n, QR + KR:], ROWS[:, NE + ROPE:NE + 2 * ROPE], ALU.mult)
            step(ins)
            dve.wait_ge(att_in, 16 * 3)

            def rotate(x):
                x = x.rearrange("p t (a b f) -> p t a b f", a=2, b=2)
                cs = [ROPT[:, s, :, :].rearrange("p t (a f) -> p t a f", a=2) for s in range(2)]
                r = [RT[:, s, :, :].rearrange("p t (a f) -> p t a f", a=2) for s in range(2)]
                for a_ in range(2):
                    x1, x2 = x[:, :, a_, 0, :], x[:, :, a_, 1, :]
                    c, s = cs[0][:, :, a_, :], cs[1][:, :, a_, :]
                    r0, r1 = r[0][:, :, a_, :], r[1][:, :, a_, :]
                    tt(r0, x2, s, ALU.mult)
                    step(tt(r1, x1, s, ALU.mult))
                    tt(x1, x1, c, ALU.mult)
                    step(tt(x2, x2, c, ALU.mult))
                    tt(x1, x1, r0, ALU.subtract)
                    step(tt(x2, x2, r1, ALU.add))

            rotate(KRT[:, 0:TT, :])
            for h in range(NH):
                for b in range(5):
                    dve.wait_ge(kv_mm, 5 * h + b + 1)
                    give(v.tensor_copy(KVT[:, 2 * b:2 * b + 2, :].rearrange("p t c -> p (t c)"), ps[:, (4 + b) % 8, :]), kv_ev)
                dve.wait_ge(hss, h + 1)
                step(tt(ST[:, 74:84], ST[:, 74:84], ST[:, 38:48], ALU.add))
                give(ts(ST[:, 84:102], ST[:, 66:84], 1.0 / QK, EPS, ALU.mult, ALU.add), hvar)
                dve.wait_ge(hstd, h + 1)
                step(v.reciprocal(ST[:, 84:102], ST[:, 84:102]))
                for i in range(TT):
                    ts(QTK[:, i, 0:NOPE], QTK[:, i, 0:NOPE], ST[:, 84 + i:85 + i], None, ALU.mult)
                    ins = stt(out=QRO[:, i, :], in0=QTK[:, i, NOPE:], scalar=ST[:, 84 + i:85 + i], in1=ROWS[:, NE:NE + ROPE],
                              op0=ALU.mult, op1=ALU.mult)
                for i in range(KT):
                    ts(KVT[:, i, 0:NOPE], KVT[:, i, 0:NOPE], ST[:, 92 + i:93 + i], None, ALU.mult)
                    ins = ts(KRH[:, i, :], KRT[:, i, :], ST[:, 92 + i:93 + i], None, ALU.mult)
                step(ins)
                rotate(QRO[:, :, :])
                give(v.memset(ST[:, 103:104], 0.0), h_ready)
                for g in (2, 3, 7, 8, 9):
                    dve.wait_ge(ht_mm, 10 * h + g + 1)
                    if g < 4:
                        give(ts(QTR[:, (g - 2) * 512:(g - 1) * 512], ps[0:64, g, :], SCALE, None, ALU.mult), ht_dve)
                    else:
                        w = 512 if g < 9 else 256
                        give(v.tensor_copy(KTR[:, (g - 7) * 512:(g - 7) * 512 + w], ps[0:64, g % 8, 0:w]), ht_dve)
                for i in range(TT + 1):
                    u = TT * h + i
                    if i < TT:
                        dve.wait_ge(s_mm, u + 1)
                        b = 3 * (u % 2)
                        step(v.tensor_reduce(ST[:, 108 + u % 2:109 + u % 2], banks(b, 3)[:, 0:KEYS], X, ALU.max))
                        give(ts(ST[:, 104 + u % 2:105 + u % 2], ST[:, 108 + u % 2:109 + u % 2], -1.0, None, ALU.mult), s_max)
                    if i:
                        dve.wait_ge(pt_mm, 3 * u - 1)
                        give(v.tensor_copy(PT[:, 4:8, :].rearrange("p a b -> p (a b)"), ps[:, 7, :]), pt_dve)
                    if i < TT:
                        dve.wait_ge(p_ready, u + 1)
                        step(v.reciprocal(ST[:, 110:111], ST[:, 106 + u % 2:107 + u % 2]))
                        give(ts(PB[u % 2][:, :], PB[u % 2][:, :], ST[:, 110:111], None, ALU.mult), p_norm)
            stage_end(dve, 5)

            for k in range(DT):
                ins = ts(SREP[:, k, :], ONE, SIL[:, k:k + 1], None, ALU.mult)
            give(ins, srep_ready)
            step(v.memset(RTW[:, 2 * NE:3 * NE], 0.0))
            step(v.memset(LPAIR[:, NE * LCOL:].bitcast(F32), 0.0))
            step(v.memset(LTOK[:, NE * LCOL:].bitcast(F32), 0.0))
            dve.wait_ge(g1_mm, 2)
            dve.wait_ge(f_in, 32)
            tt(G1B[:, :], banks(0), G1R[:, :], ALU.add)
            dve.wait_ge(mod2_mm, 6)
            src = ps[:, 2, 0:48].rearrange("p (m k s) -> p m k s", m=3, s=2)
            step(tt(MODC[:, 2:5, :, 0], src[:, :, :, 0], PAR[:, mb + 24:mb + 48].rearrange("p (m k) -> p m k", m=3), ALU.add))
            give(stt(out=A2[:, :], in0=MODC[:, 3, :, 0], scalar=1.0, in1=PAR[:, COLS["norm2"]:COLS["norm2"] + 8],
                op0=ALU.add, op1=ALU.mult), mod2_ready)
            dve.wait_ge(mod2_ready, 1)

            W = lambda n, w=1: RTW[:, 8 * NE + n:8 * NE + n + w]

            def residual(i):
                dve.wait_ge(wo_mm, i + 1)
                dve.wait_ge(xo_in[i % 2], 16 * (i // 2 + 1))
                if i >= 2:
                    dve.wait_ge(xnew_out[i % 2], 16 * (i // 2))
                step(tt(XNEW[:, i % 2, :], banks(2 * (i % 2)), G1B[:, :], ALU.mult))
                give(tt(XNEW[:, i % 2, :], XNEW[:, i % 2, :], XIN[i % 2][:, :], ALU.add), xnew_ready)
                dve.wait_ge(fss, i + 1)
                give(ts(ST[:, 10 + i:11 + i], ST[:, i:i + 1], 1.0 / D, EPS, ALU.mult, ALU.add), fvar)
                dve.wait_ge(fstd, i + 1)
                step(v.reciprocal(ST[:, 10 + i:11 + i], ST[:, 10 + i:11 + i]))
                if i >= 2:
                    dve.wait_ge(xn_out[i % 2], 16 * (i // 2))
                give(ts(XNB[i % 2][:, :], XNEW[:, i % 2, :], ST[:, 10 + i:11 + i], None, ALU.mult), fxn)

            def choose(i):
                dve.wait_ge(ft_mm, 2 * i + 2)
                for j in range(4):
                    ins = ts(H2T[i % 2][:, 4 + j, :], ps[:, 5, j * P:(j + 1) * P], A2[:, 4 + j:5 + j],
                             MODC[:, 2, 4 + j, 0:1], ALU.mult, ALU.add)
                give(ins, ft_dve)
                dve.wait_ge(lg_mm, i + 1)
                step(tt(RTW[:, 0:NE], ps[:, 6, 0:NE], ROWS[:, 0:NE], ALU.add))
                step(v.max(W(0, 8), RTW[:, 0:NE]))
                step(v.max_index(W(8, 8).bitcast(mybir.dt.uint32), W(0, 8), RTW[:, 0:NE]))
                give(ts(W(24), W(0), -1.0, None, ALU.mult), gneg)
                step(v.tensor_copy(W(32, 8), W(8, 8).bitcast(mybir.dt.uint32)))
                for k in range(TOPK):
                    step(ts(RTW[:, (4 + k) * NE:(5 + k) * NE], IOTA, W(32 + k), None, ALU.is_equal))
                step(tt(RTW[:, 3 * NE:4 * NE], RTW[:, 4 * NE:5 * NE], RTW[:, 5 * NE:6 * NE], ALU.add))
                step(tt(RTW[:, NE:2 * NE], RTW[:, 6 * NE:7 * NE], RTW[:, 7 * NE:8 * NE], ALU.add))
                give(tt(RTW[:, NE:2 * NE], RTW[:, NE:2 * NE], RTW[:, 3 * NE:4 * NE], ALU.add), route_m)
                dve.wait_ge(rk_mm, i + 1)
                step(tt(RTW[:, 3 * NE:4 * NE], ps[:, 7, 0:NE], EBASE, ALU.add))
                step(tt(RTW[:, 2 * NE:3 * NE], RTW[:, 2 * NE:3 * NE], RTW[:, NE:2 * NE], ALU.add))
                for k in range(TOPK):
                    step(tt(RTW[:, 0:NE], RTW[:, (4 + k) * NE:(5 + k) * NE], RTW[:, 3 * NE:4 * NE], ALU.mult))
                    step(v.tensor_reduce(W(40 + k), RTW[:, 0:NE], X, ALU.add))
                dve.wait_ge(gexp, i + 1)
                step(v.reciprocal(W(26), W(25)))
                ts(GATE[:, i, :], W(16, 4), W(26), None, ALU.mult)
                give(v.tensor_copy(SLOTI[:, i, :], W(40, 4)), slot_ready)
                dve.wait_ge(slot_ready, i + 1)

            for i in range(TT + 1):
                if i < TT:
                    residual(i)
                if i:
                    choose(i - 1)
            dve.wait_ge(cnt_mm, 1)
            v.tensor_reduce(W(50), ps[:, 7, 0:NE], X, ALU.max)
            step(v.tensor_copy(CNT[:, 0:NE], ps[:, 7, 0:NE]))
            give(v.tensor_copy(CNT[:, NE:NE + 1], W(50)), cnt_ready)
            dve.wait_ge(list_mm, 1)
            v.memset(W(0), 0.0)
            step(v.tensor_copy(LPAIR[:, 0:NE * LCOL], ps[:, 6, 0:NE * LCOL]))
            give(ts(LTOK[:, 0:NE * LCOL], LPAIR[:, 0:NE * LCOL], 2, None, ALU.logical_shift_right), list_ready)
            stage_end(dve, 6)

            v.memset(XSR[:, :, :], 0.0).then_inc(rows_init, 1)
            v.memset(YR[:, :, :], 0.0).then_inc(rows_init, 1)
            dve.wait_ge(rows_init, 2)
            dve.sem_inc(gu_evac, 4)
            dve.sem_inc(yt_ready, 2)

            def one(it, e, block, count, count_next):
                def times_sigmoid(w, half, m):
                    n = 4 * half + m
                    dve.wait_ge(sg_ready, it * 8 + n + 1)
                    tt(TG[:, m, 0:w], GA[:, m % 2, 0:w], SG[:, m % 2, 0:w], ALU.mult).then_inc(tg_step, 1)
                    dve.wait_ge(tg_step, it * 8 + n + 1)

                def body(w):
                    for half in range(2):
                        for m in range(4):
                            t = 8 * half + m
                            dve.wait_ge(gu_done, it * 16 + t + 1)
                            ts(GA[:, m % 2, 0:w], ps[:, m, 0:w], BGU[:, bass.ds(e * 16 + 4 * half + m, 1)], LIMIT,
                               ALU.add, ALU.min).then_inc(gu_evac, 1)
                            dve.wait_ge(gu_evac, it * 16 + 4 + t + 1)
                            if m:
                                times_sigmoid(w, half, m - 1)
                        times_sigmoid(w, half, 3)
                        for m in range(4):
                            t = 8 * half + 4 + m
                            n = 4 * half + m
                            dve.wait_ge(gu_done, it * 16 + t + 1)
                            ts(U1[:, 0:w], ps[:, m, 0:w], BGU[:, bass.ds(e * 16 + 8 + n, 1)], LIMIT,
                               ALU.add, ALU.min).then_inc(gu_evac, 1)
                            dve.wait_ge(gu_evac, it * 16 + 4 + t + 1)
                            ts(U1[:, 0:w], U1[:, 0:w], -LIMIT, 1.0, ALU.max, ALU.add).then_inc(u1_step, 1)
                            dve.wait_ge(u1_step, it * 8 + n + 1)
                            tt(HE[:, n, 0:w], U1[:, 0:w], TG[:, m, 0:w], ALU.mult).then_inc(he_ready, 1)
                            dve.wait_ge(he_ready, it * 8 + n + 1)
                    for d in range(DT):
                        dve.wait_ge(y_done, it * 8 + d + 1)
                        ts(YT[:, d, 0:w], ps[:, 4 + d % 2, 0:w], BDN[:, bass.ds(e * 8 + d, 1)], MODC[:, 4, d, 0:1],
                           ALU.add, ALU.mult).then_inc(yt_ready, 1)
                by_width(dve, count, (128, 256, 384, 512), body)

            passes(dve, one)
            stage_end(dve, 7)
            for i in range(TT):
                dve.wait_ge(yq_in[i % 2], 32 * (i // 2 + 1))
                for k in range(TOPK):
                    ins = stt(out=XR[i % 2][:, :], in0=YQ[i % 2][:, k, :], scalar=GATE[:, i, k:k + 1], in1=XR[i % 2][:, :],
                              op0=ALU.mult, op1=ALU.add)
                    if k < TOPK - 1:
                        ins.then_inc(sum_step, 1)
                        dve.wait_ge(sum_step, 3 * i + k + 1)
                give(ins, sum_ready)

        @block.gpsimd
        def _(pool):
            g = nc.gpsimd
            for n in range(1, 6):
                stage_end(pool, n)
            g.memset(LF[:, :], float(NOPAIR)).then_inc(list_fill, 1)
            pool.wait_ge(list_fill, 1)
            pool.dma_start(list_d.rearrange("(p f) o -> p (f o)", p=P), LF[:, :]).then_inc(list_init, 16)
            pool.wait_ge(list_init, 16)
            for i in range(TT):
                pool.wait_ge(slot_ready, i + 1)
                for k in range(TOPK):
                    n = i * TOPK + k
                    g.indirect_dma_start(out=list_d, out_offset=bass.IndirectOffsetOnAxis(ap=SLOTI[:, i, k:k + 1], axis=0),
                                         in_=PIDS[:, n:n + 1], in_offset=None).then_inc(list_out, 16)
            pool.wait_ge(list_out, 16 * PAIRS // P)
            lv = list_d.rearrange("(g r c) o -> g r (c o)", g=2, c=P)
            for h in range(2):
                pool.dma_start(JF[:, h * P:(h + 1) * P], lv[h]).then_inc(list_in, 16)
            stage_end(pool, 6)

            pool.wait_ge(cnt_ready, 1)
            pool.wait_ge(rows_init, 2)
            pool.sem_inc(yr_free, 1)
            LAST_TOK, LAST_PAIR = T - 1, PAIRS - 1

            def gather(number, column):
                g.tensor_copy(IXG[:, :], LTOK[:, bass.ds(column, NB)]).then_inc(ix_step, 1)
                pool.wait_ge(ix_step, number * 2 + 1)
                pool.sem_inc(pool_mark, 1)
                for b in range(NB):
                    g.indirect_dma_start(out=XSR[:, b, :], out_offset=None, in_=xn_d,
                                         in_offset=bass.IndirectOffsetOnAxis(ap=IXG[:, b:b + 1], axis=0),
                                         bounds_check=LAST_TOK, oob_is_err=False).then_inc(xs_in[b], 16)

            def one(it, e, block, count, count_next):
                pool.wait_ge(tp_done, it * 16 + 8)
                gather(it + 1, e * LCOL + NB if block else (e + 1) * LCOL)
                g.tensor_copy(IXS[:, :], LPAIR[:, bass.ds(e * LCOL + NB * block, NB)]).then_inc(ix_step, 1)
                pool.wait_ge(ix_step, it * 2 + 4)
                pool.wait_ge(tp_evac, it * 16 + 26)
                pool.sem_inc(pool_mark, 1)
                for b in range(NB):
                    g.indirect_dma_start(out=y_d, out_offset=bass.IndirectOffsetOnAxis(ap=IXS[:, b:b + 1], axis=0),
                                         in_=YR[:, b, :], in_offset=None,
                                         bounds_check=LAST_PAIR, oob_is_err=False).then_inc(y_out[b], 16)
                for b in range(NB):
                    pool.wait_ge(y_out[b], it * 16 + 16)
                pool.sem_inc(yr_free, 1)

            gather(0, 0)
            pool.sem_inc(ix_step, 1)
            passes(pool, one)
            stage_end(pool, 7)


_OUT = "out"


def kernel(**inputs):
    import concourse.bacc as bacc
    from concourse.bass_utils import run_bass_kernel_spmd

    v = {n: np.asarray(x) for n, x in inputs.items()}
    arrays = {**constants(), **layout(v)}
    nc = bacc.Bacc("TRN2", target_bir_lowering=False, num_devices=1)
    args = {n: nc.dram_tensor(n + "_dram", x.shape, mybir.dt.from_np(x.dtype), kind="ExternalInput").ap()
            for n, x in arrays.items()}
    out = nc.dram_tensor(_OUT, (T, D), F32, kind="ExternalOutput").ap()
    build(nc, args, out)
    r = run_bass_kernel_spmd(nc, [{n + "_dram": x for n, x in arrays.items()}], core_ids=[0])
    return r.results[0][_OUT].reshape(1, T, D)
```

```python
import math
from contextlib import ExitStack

import numpy as np
import concourse.bass as bass
from concourse import mybir

F32 = mybir.dt.float32
I32 = mybir.dt.int32
ALU = mybir.AluOpType
ACT = mybir.ActivationFunctionType
X = mybir.AxisListType.X

P = 128
D = 1024
DT = D // P
T = 1024
TT = T // P
CTX = 256
CT = CTX // P
KT = TT + CT
KEYS = T + CTX
HY = 512
HC = HY // P
NH = 4
NOPE, ROPE, VD = 128, 64, 128
QK = NOPE + ROPE
QR, KR = 256, 128
LAT = QR + KR + ROPE
INC = 3 * HY + LAT
NE, TOPK, FF = 32, 4, 1024
EPS = 1e-6
SCALE = QK ** -0.5
PAIRS = T * TOPK
CAP = T
BLK = 512
NB = BLK // P
LCOL = CAP // P
NOTOKEN = 4 * T
MAGIC = 1.5 * 2.0 ** 23
GRID_W, THETA = 64, 10000.0

FACTORS = [(3 * math.pi / 4 / 256, 2 * math.pi / 256, 256, 4),
           (math.pi / 4 / 256, 2 * math.pi / 256, 256, 4),
           (math.pi / 512, 2 * math.pi / 512, 256, 4),
           (math.pi / 256, 2 * math.pi / 256, 128, 2),
           (0.0, 2 * math.pi / 256, 128, 2)]
PAIR_TILES = [(0, 4), (0, 4), (4, 4), (4, 4), (8, 4), (8, 4), (12, 2), (14, 2)]
UNIT0 = [0, 8, 16, 24, 32, 40, 48, 52]
UNITS = 56
SPLIT = 24
ORDER = (4, 5, 6, 7, 3, 0, 1, 2)

COLS = {}


def _cols():
    at = 0
    for name, n in (("c", 16), ("norm1", 8), ("norm2", 8), ("convw", 36), ("convb", 12), ("qn", 2), ("kvn", 1),
                    ("modb", 48), ("freq", 1), ("b1", 1), ("b2", 1), ("b3", 1), ("gq", 1), ("gk", 1)):
        COLS[name] = at
        at += n
    return at


NPAR = _cols()


def constants():
    t = np.linspace(0.0, 1.0, T, dtype=np.float32)
    bands = 16
    w_ang = (2.0 * math.pi * np.arange(T, dtype=np.float32) / T).astype(np.float32)
    f = np.linspace(1e-4, bands - 1, bands, dtype=np.float32)
    ang = (f[None, :] * w_ang[:, None]).astype(np.float32)
    z = np.concatenate([t[:, None], np.cos(ang), -np.sin(ang)], axis=1).astype(np.float32)
    back = np.r_[0, np.arange(T - 1, 0, -1)]
    z2 = np.concatenate([z.T, z[back].T], axis=0)
    lo, hi = math.log(1e-2) / 0.3, math.log(1e-2) / 1.5
    deltas = np.abs(np.linspace(lo, hi, HY, dtype=np.float32))
    decay = np.exp(-t[:, None] * deltas[None, :]).astype(np.float32)
    dec = np.stack([decay, decay[back]], axis=1).reshape(TT, P, 2, HY).transpose(1, 0, 2, 3)
    angles, fwd = [], np.zeros((P, UNITS, P), np.float64)
    for a0, step, n, tiles in FACTORS:
        angles.append(a0 + step * np.arange(n))
    theta = np.concatenate(angles)
    unit = 0
    for pair, (_, tiles) in enumerate(PAIR_TILES):
        th = theta[pair * P:(pair + 1) * P]
        for ri in range(2):
            for k in range(tiles):
                n = k * P + np.arange(P)
                a = n[:, None] * th[None, :]
                m = np.cos(a) if ri == 0 else np.sin(a)
                if pair == 7 and ri == 1:
                    m[:, 0] = (-1.0) ** n
                fwd[:, unit, :] = m
                unit += 1
    n = np.arange(T)
    inv = np.zeros((P, 16, T), np.float64)
    for pair in range(8):
        a = theta[pair * P:(pair + 1) * P][:, None] * n[None, :]
        inv[:, 2 * pair] = np.cos(a) * 2 / 2048
        inv[:, 2 * pair + 1] = np.sin(a) * 2 / 2048
    inv[0, 14] = 1.0 / 2048
    inv[0, 15] = (-1.0) ** n / 2048
    row, col = (np.arange(T) // GRID_W).astype(np.float32), (np.arange(T) % GRID_W).astype(np.float32)
    nf = ROPE // 4
    invf = np.power(np.float32(THETA), -np.arange(nf, dtype=np.float32) / nf).astype(np.float32)
    ra = np.stack([row[:, None] * invf, col[:, None] * invf], axis=1).astype(np.float32)
    rope = np.stack([np.cos(ra), np.sin(ra)]).reshape(2, TT, P, 32).transpose(2, 0, 1, 3)
    small = np.zeros((P, 3 * P + NE + NE + 4 * TT), np.float32)
    small[:, 0:P] = np.eye(P)
    small[:, P:2 * P] = np.triu(np.ones((P, P)), 1)
    small[:, 2 * P:3 * P] = 1.0
    small[:, 3 * P:3 * P + NE] = np.arange(NE)
    small[:, 3 * P + NE:3 * P + 2 * NE] = np.arange(NE) * CAP
    ids = np.arange(TT)[None, :, None] * P + np.arange(P)[:, None, None] + 0 * np.arange(TOPK)
    small[:, 3 * P + 2 * NE:] = ids.reshape(P, TT * TOPK)
    c = np.ascontiguousarray
    return {"k_z": c(z2), "k_decay": c(dec), "k_fwd": c(fwd.astype(np.float32)),
            "k_inv": c(inv.astype(np.float32)), "k_rope": c(rope.astype(np.float32)), "k_small": small}


def layout(v):
    c = np.ascontiguousarray
    col = lambda a: np.asarray(a).reshape(-1, P).T
    two = lambda a: np.concatenate([a, a])[:, None]
    par = [col(v["c"]), col(v["c_ctx"]), col(v["norm1_g"]), col(v["norm2_g"]), col(v["hy_conv_w"]),
           col(v["hy_conv_b"]), col(v["mla_q_norm_g"]), col(v["mla_kv_norm_g"]), col(v["mod_b"]),
           two(v["hy_f_freq"][0]), two(v["hy_f_b1"][0]), two(v["hy_f_b2"][0]), two(v["hy_f_b3"][0]),
           v["qk_norm_q_g"][0][:NOPE, None], v["qk_norm_k_g"][0][:NOPE, None]]
    fw = np.zeros((P, 3 * P + HY), np.float32)
    for i, n in enumerate(("hy_f_w1", "hy_f_w2", "hy_f_w3")):
        w = v[n][0]
        r = w.shape[0]
        fw[0:r, i * P:i * P + 64] = w
        fw[r:2 * r, i * P + 64:(i + 1) * P] = w
    fw[0:64, 3 * P:] = v["hy_f_w4"][0][:, :HY]
    fw[64:, 3 * P:] = v["hy_f_w4"][0][:, HY:]
    rows = np.concatenate([v["mod_b"][0, 2 * D:3 * D], v["router_b"][0], v["qk_norm_q_g"][0][NOPE:],
                           v["qk_norm_k_g"][0][NOPE:]])
    return {"x": c(v["x"][0]), "ctx": c(v["ctx"][0]), "mod_w": c(v["mod_w"][0]), "w_in": c(v["w_in"][0]),
            "par": c(np.concatenate(par, axis=1)), "fw": fw, "hy_bias": c(v["hy_bias"]),
            "rows": c(np.broadcast_to(rows, (P, rows.size))),
            "w_uq": c(v["mla_w_uq"][0]), "w_ukv": c(v["mla_w_ukv"][0]), "w_out": c(v["w_out"][0]),
            "router_w": c(v["router_w"][0]), "w_gu": c(v["exp_w_gu"][0]), "w_down": c(v["exp_w_down"][0]),
            "b_gu": c(v["exp_b_gu"][0].reshape(NE * 16, P).T), "b_dn": c(v["exp_b_down"][0].reshape(NE * 8, P).T)}


KB = 1024
RING0 = 16512
SLOT = 16 * KB
WORK0 = RING0 + 4 * SLOT
PERS0 = 229344 - 12 * KB
FRONT_CHUNKS = 26
WIDTHS = (96, 128, 160, 192, 224, 256, 288, 320, 352, 384, 416, 448, 512)
BLOCKS = tuple(range(P, BLK + 1, P))
USES = [sum(j % 4 == i for j in range(FRONT_CHUNKS)) for i in range(4)] + [0, 0]
WSLOT = (2, 3, 0, 1, 4, 5)
LIMIT = 7.0
ALPHA = 1.702


def build(nc, a, out):
    S = ExitStack()

    def at(name, kb, shape, dt=F32, base=WORK0):
        return nc.alloc_sbuf_tensor_at(name, shape, dt, offset=base + int(kb * KB))

    def dram(name, shape, dt=F32):
        return nc.dram_tensor(name, shape, dt, kind="Internal").ap()

    with S:
        def sem(name):
            return S.enter_context(nc.semaphore(name))

        ring = [at(f"ring{i}", 0, [P, 8, 512], base=RING0 + i * SLOT) for i in range(6)]
        SD = at("SD", 0, [P, 16, HY])
        RES = at("RES", 32, [P, 16, HY])
        TMP = at("TMP", 64, [P, 4, HY])
        DEC = at("DEC", 72, [P, TT, 2, HY])
        ZS = at("ZS", 104, [66, T])
        HA = at("HA", 108, [P, T])
        HB = at("HB", 112, [P, T])
        RN = at("RN", 116, [P, T])
        FW = at("FW", 120, [P, 3 * P + HY])
        AB = [at("AB0", 124, [P, 2, HY]), at("AB1", 64, [P, 2, HY])]
        ABS = [at("ABS0", 68, [P, 2, HY]), at("ABS1", 112, [P, 2, HY])]
        BIAS = at("BIAS", 128, [1, HY])
        HT = at("HT", 32, [P, DT, T])
        HTC = at("HTC", 64, [P, DT, CTX])
        XB = [at("XB0", 72, [P, 4, D]), at("XB1", 88, [P, 4, D])]
        JUNK = at("JUNK", 108, [P, D])
        VTOK = at("VTOK", 72, [P, TT, HY])
        X0T = at("X0T", 88, [P, HC, T])
        X1T = at("X1T", 104, [P, HC, T])
        VTMP = [at("VT0", 122, [P, T]), at("VT1", 126, [P, T])]
        LATB = at("LATB", 104, [P, KT, LAT])
        RESV = at("RESV", 32, [P, 16, HY])
        TMPV = at("TMPV", 64, [P, 4, HY])
        PR = at("PR", 122, [P, 4, HY])
        CQT = at("CQT", 0, [P, 2, T])
        CKT = at("CKT", 8, [P, KEYS])
        KRT = at("KRT", 13, [P, KT, ROPE])
        WUQ = at("WUQ", 16, [P, 2, NH * QK])
        WUKV = at("WUKV", 22, [P, NH * 256])
        ROPT = at("ROPT", 26, [P, 2, TT, 32])
        KVT = at("KVT", 28, [P, KT, 256])
        QTK = at("QTK", 38, [P, TT, QK])
        KRH = at("KRH", 44, [P, KT, ROPE])
        KTN = at("KTN", 47, [P, KEYS])
        KTR = at("KTR", 52, [64, KEYS])
        QTN = at("QTN", 57, [P, T])
        QTR = at("QTR", 61, [64, T])
        PB = [at("PB0", 65, [P, KEYS]), at("PB1", 70, [P, KEYS])]
        PT = at("PT", 75, [P, KT, P])
        RT = at("RT", 81, [P, 2, TT, 32])
        QRO = at("QRO", 83, [P, TT, ROPE])
        JE = at("JE", 130.5, [P, QR])
        SREP = at("SREP", 122, [P, DT, P])
        G1B = at("G1B", 126, [P, D])
        YA = at("YA", 104, [P, NH, T])
        XIN = [at("XIN0", 4, [P, D]), at("XIN1", 8, [P, D])]
        XNB = [at("XNB0", 12, [P, D]), at("XNB1", 16, [P, D])]
        JF = at("JF", 20, [P, D])
        H2T = [at("H2T0", 24, [P, DT, P]), at("H2T1", 28, [P, DT, P])]
        RW = at("RW", 62, [P, DT, NE])
        XNEW = at("XNEW", 54, [P, 2, D])
        LF = at("LF", 64, [P, NE * LCOL, 2])
        XSR = at("XSR", 32, [P, NB, D])
        XST = at("XST", 48, [P, DT, BLK])
        HE = at("HE", 64, [P, DT, BLK])
        YT = at("YT", 80, [P, DT, BLK])
        TG = at("TG", 96, [P, 4, BLK])
        GA = at("GA", 104, [P, 2, BLK])
        SG = at("SG", 108, [P, 2, BLK])
        U1 = at("U1", 112, [P, BLK])
        YR = at("YR", 114, [P, NB, D])
        pers = [0]

        def keep(name, shape, dt=F32):
            n = 4 * int(np.prod(shape[1:]))
            t = nc.alloc_sbuf_tensor_at(name, shape, dt, offset=PERS0 + pers[0])
            pers[0] += (n + 31) // 32 * 32
            assert PERS0 + pers[0] <= 229344, name
            return t

        SM = keep("SM", [P, 3 * P + 2 * NE + 4 * TT])
        ID, TRI, ONE = SM[:, 0:P], SM[:, P:2 * P], SM[:, 2 * P:3 * P]
        IOTA, EBASE = SM[:, 3 * P:3 * P + NE], SM[:, 3 * P + NE:3 * P + 2 * NE]
        TOKENS = SM[:, 3 * P + 2 * NE:]
        PAR = keep("PAR", [P, NPAR])
        ROWS = keep("ROWS", [P, NE + 2 * ROPE])
        SIL = keep("SIL", [P, 16])
        MODC = keep("MODC", [P, 5, DT, 2])
        A1 = keep("A1", [P, DT, 2])
        A2 = keep("A2", [P, DT])
        RNC = keep("RNC", [P, HC])
        ST = keep("ST", [P, 128])
        FB = keep("FB", [P, 4])
        BGU = keep("BGU", [P, NE * 16])
        BDN = keep("BDN", [P, NE * 8])
        PAIR = keep("PAIR", [P, TT * TOPK, 2])
        SLOTI = keep("SLOTI", [P, TT, TOPK], I32)
        CNT = keep("CNT", [P, NE + 2], I32)
        LGATE = keep("LGATE", [P, NE * LCOL])
        LTOK = keep("LTOK", [P, (NE + 1) * LCOL], I32)
        IXG = keep("IXG", [P, NB], I32)
        GATES = keep("GATES", [P, NB])
        IXS = keep("IXS", [P, NB], I32)
        RTW = keep("RTW", [P, 8 * NE + 64])

        ps = S.enter_context(nc.psum_tensor("ps", [P, 8, 512], F32))

        def banks(b, n=2):
            return ps[:, b:b + n, :].rearrange("p b f -> p (b f)")

        xn_d = dram("xn_d", [T, D])
        list_d = dram("list_d", [NE * CAP, 2])

        full = [sem(f"slot_full{i}") for i in range(6)]
        free = [sem(f"slot_free{i}") for i in range(6)]
        filt_in, par_in, stage, dve_step, act_step = map(sem, ("filt_in", "par_in", "stage", "dve_step", "act_step"))
        mlp_mm, mlp_arg, mlp_sin, fk_mm, fk_done, norm_mm, kres, ku_mm, kev = map(sem, (
            "mlp_mm", "mlp_arg", "mlp_sin", "fk_mm", "fk_done", "norm_mm", "kres", "ku_mm", "kev"))
        sil_in, sil_ready, mod_mm, mod_ready = map(sem, ("sil_in", "sil_ready", "mod_mm", "mod_ready"))
        x_in = [sem(f"x_in{g}") for g in range(3)]
        ssq_ready, var_ready, std_ready, xn_ready, tp_mm, tp_act, tp_dve = map(sem, (
            "ssq_ready", "var_ready", "std_ready", "xn_ready", "tp_mm", "tp_act", "tp_dve"))
        cv_mm, cv_act, cv_done, v_ready, vt_mm, vt_ev, lat_mm, lat_ev = map(sem, (
            "cv_mm", "cv_act", "cv_done", "v_ready", "vt_mm", "vt_ev", "lat_mm", "lat_ev"))
        vres, u_mm, y_prod, inv_mm = map(sem, ("vres", "u_mm", "y_prod", "inv_mm"))
        att_in, lss, lvar, lstd, ln_ready, lt_mm, lt_ev = map(sem, (
            "att_in", "lss", "lvar", "lstd", "ln_ready", "lt_mm", "lt_ev"))
        q_mm, kv_mm, q_ev, kv_ev, hss, hvar, hstd, h_ready, ht_mm, ht_act, ht_dve = map(sem, (
            "q_mm", "kv_mm", "q_ev", "kv_ev", "hss", "hvar", "hstd", "h_ready", "ht_mm", "ht_act", "ht_dve"))
        s_mm, s_max, p_ready, p_norm, pt_mm, pt_act, pt_dve, o_mm, y_ev = map(sem, (
            "s_mm", "s_max", "p_ready", "p_norm", "pt_mm", "pt_act", "pt_dve", "o_mm", "y_ev"))
        f_in, srep_ready, g1_mm, mod2_mm, wo_mm, xnew_ready, fss, fvar, fstd, fxn = map(sem, (
            "f_in", "srep_ready", "g1_mm", "mod2_mm", "wo_mm", "xnew_ready", "fss", "fvar", "fstd", "fxn"))
        c_in, ab_ready, abs_done, norm_row, norm_col = map(sem, ("c_in", "ab_ready", "abs_done", "norm_row", "norm_col"))
        xo_in = [sem(f"xo_in{i}") for i in range(2)]
        xn_out = [sem(f"xn_out{i}") for i in range(2)]
        xnew_out = [sem(f"xnew_out{i}") for i in range(2)]
        xs_in, y_out, rows_ready = sem("xs_in"), sem("y_out"), sem("rows_ready")
        rows_init, gu_done, gu_evac, sg_ready, tg_step, he_ready, y_done, yt_ready, tp_done, tp_evac, yr_free, ix_step = map(sem, (
            "rows_init", "gu_done", "gu_evac", "sg_ready", "tg_step", "he_ready", "y_done", "yt_ready", "tp_done", "tp_evac", "yr_free", "ix_step"))
        gates_ready = sem("gates_ready")
        pool_mark = sem("pool_mark")
        ft_mm, ft_act, ft_dve, lg_mm, route_m, rk_mm, gexp, gneg, slot_ready, cnt_mm, cnt_ready = map(sem, (
            "ft_mm", "ft_act", "ft_dve", "lg_mm", "route_m", "rk_mm", "gexp", "gneg", "slot_ready", "cnt_mm", "cnt_ready"))
        list_fill, list_init, list_out, list_in, list_mm, list_ready = map(sem, (
            "list_fill", "list_init", "list_out", "list_in", "list_mm", "list_ready"))

        block = S.enter_context(nc.Block())

        def stage_end(eng, n):
            eng.drain().then_inc(stage, 1)
            eng.wait_ge(stage, 4 * n)

        def by_width(eng, count, widths, body):
            if len(widths) == 1:
                body(widths[0])
                return
            half = len(widths) // 2
            with eng.If(count < widths[half - 1] + 1):
                by_width(eng, count, widths[:half], body)
            with eng.Else():
                by_width(eng, count, widths[half:], body)

        def passes(eng, one, counts=True):
            def load(col):
                return eng.value_load(CNT[0:1, bass.ds(col, 1)], min_val=0, max_val=CAP)

            if counts:
                this = eng.alloc_register("this_count")
                eng.reg_mov(this, load(0))
            with eng.Fori(0, NE // 2) as pair:
                for half in range(2):
                    e = eng.snap(2 * pair + half, min_val=0, max_val=NE - 1)
                    if counts:
                        count_next = load(e + 1)
                        one(e, e, 0, eng.snap(this, min_val=0, max_val=CAP), count_next)
                        eng.reg_mov(this, count_next)
                    else:
                        one(e, e, 0, None, None)
            eng.wait_ge(cnt_ready, 1)
            most = eng.value_load(CNT[0:1, NE + 1:NE + 2], min_val=0, max_val=CAP)
            with eng.If(most > BLK):
                number = eng.alloc_register("pass_number")
                eng.reg_mov(number, NE)
                with eng.Fori(0, NE) as e:
                    c = load(e)
                    with eng.If(c > BLK):
                        it = eng.snap(number, min_val=NE, max_val=2 * NE)
                        one(it, e, 1, c - BLK, c - BLK)
                        eng.reg_add(number, number, 1)

        @block.sync
        def _(sp):
            mod = a["mod_w"].rearrange("(k p) n -> p k n", p=P)
            win = a["w_in"].rearrange("(k p) n -> p k n", p=P)
            wout = a["w_out"].rearrange("(k p) n -> p k n", p=P)
            fwd = [(SPLIT, UNITS), (0, SPLIT)]
            chunks = [("mod", n) for n in (0, 1, 2, 3)] + [("fwd", n) for n in range(2)] + \
                [("in", n) for n in range(4)] + [("fwd", n) for n in range(2)] + [("inv", n) for n in range(4)] + \
                [("mod", n) for n in (4, 5, 6, 7, 8, 9, 10, 11)] + [("out", n) for n in range(2)]
            assert len(chunks) == FRONT_CHUNKS
            for j, (kind, n) in enumerate(chunks):
                slot = ring[j % 4]
                if j == 0:
                    sp.wait_ge(filt_in, 16 * 3)
                if j >= 4:
                    sp.wait_ge(free[j % 4], j // 4)
                if kind == "fwd":
                    u0, u1 = fwd[n]
                    dst = slot[:, :, :].rearrange("p a b -> p (a b)")[:, 0:(u1 - u0) * P]
                    src = a["k_fwd"][:, u0:u1, :].rearrange("p u m -> p (u m)")
                elif kind == "inv":
                    dst = slot[:, :, :].rearrange("p a b -> p (a b)")
                    src = a["k_inv"][:, 4 * n:4 * n + 4, :].rearrange("p u m -> p (u m)")
                elif kind == "in" and n == 3:
                    dst, src = slot[:, :, 0:LAT], win[:, :, 3 * HY:INC]
                else:
                    dst, src = slot[:, :, :], {"mod": mod, "in": win, "out": wout}[kind][:, :, n * 512:(n + 1) * 512]
                sp.dma_start(dst, src).then_inc(full[j % 4], 16)
            def weights(it, e, block, count, count_next):
                gu = a["w_gu"][bass.ds(e, 1), :, :].rearrange("o (k p) n -> p (o k) n", p=P)
                dn = a["w_down"][bass.ds(e, 1), :, :].rearrange("o (k p) n -> p (o k) n", p=P)
                for c in range(6):
                    src = gu[:, :, FF * (c % 2) + 512 * (c // 2):][:, :, 0:512] if c < 4 else dn[:, :, 512 * (c - 4):][:, :, 0:512]
                    slot = WSLOT[c]
                    sp.wait_ge(free[slot], it + (USES[slot] if c < 4 else 1))
                    sp.dma_start(ring[slot][:, :, :], src).then_inc(full[slot], 16)

            passes(sp, weights, False)

        def arrived(pe, j):
            pe.wait_ge(full[j % 4], 16 * (j // 4 + 1))

        @block.tensor
        def _(pe):
            mm = nc.tensor.matmul
            pe.wait_ge(filt_in, 16 * 3)

            def mod_columns(chunk, col, bank, done):
                arrived(pe, chunk)
                for m in range(4):
                    for k in range(DT):
                        ins = mm(ps[:, bank, 2 * (col + m):2 * (col + m) + 2], ring[chunk % 4][:, k, m * P:(m + 1) * P],
                                 SIL[:, k:k + 9:8], start=k == 0, stop=k == DT - 1)
                ins.then_inc(done, 1)

            for l in range(3):
                if l:
                    pe.wait_ge(mlp_sin, l)
                for h in range(2):
                    src = (ZS, HA, HB)[l]
                    rows = 66 if l == 0 else P
                    mm(ps[:, h, :], FW[0:rows, l * P:(l + 1) * P], src[0:rows, h * 512:(h + 1) * 512],
                       start=True, stop=True).then_inc(mlp_mm, 1)
                if l == 1:
                    pe.wait_ge(sil_ready, 1)
                for q in ((), (0,), (1,))[l]:
                    mod_columns(q, 4 * q, 7, mod_mm)
                    pe.wait_ge(mod_mm, q + 1)
                    pe.sem_inc(free[q], 1)
            pe.wait_ge(mlp_sin, 3)
            def sum_abs(i):
                pe.wait_ge(abs_done, i + 1)
                for r in range(2):
                    ins = mm(ps[0:1, 4, :], ONE[:, 0:1], ABS[i % 2][:, r, :], start=i == 0 and r == 0,
                             stop=i == TT - 1 and r == 1)
                ins.then_inc(norm_mm, 1)

            for i in range(TT):
                if i >= 2:
                    pe.wait_ge(fk_done, i - 1)
                b = 2 * (i % 2)
                mm(ps[:, b, :], HA[0:64, i * P:(i + 1) * P], FW[0:64, 3 * P:], start=True, stop=True)
                mm(ps[:, b + 1, :], HA[64:P, i * P:(i + 1) * P], FW[64:P, 3 * P:], start=True, stop=True).then_inc(fk_mm, 1)
                if i in (3, 5):
                    q = i // 2 + 1
                    mod_columns(q, 4 * q, 7, mod_mm)
                    pe.wait_ge(mod_mm, q + 1)
                    pe.sem_inc(free[q], 1)
                if i:
                    sum_abs(i - 1)
            sum_abs(TT - 1)
            pe.wait_ge(norm_row, 1)
            for c in range(HC):
                ins = mm(ps[:, 5, c:c + 1], RN[0:1, HY + c * P:HY + (c + 1) * P], ONE[0:1, 0:1], start=True, stop=True)
            ins.then_inc(norm_col, 1)

            def transforms(res, first_chunk, ready, ring_wait, done):
                pe.wait_ge(ready, 1)
                arrived(pe, first_chunk)
                for pos, pair in enumerate(ORDER):
                    k0, tiles = PAIR_TILES[pair]
                    if pos == 4:
                        pe.wait_ge(ready, 2)
                    if pos == 5:
                        arrived(pe, first_chunk + 1)
                    ring_wait(pos)
                    u = UNIT0[pair]
                    w = ring[(first_chunk + (u < SPLIT)) % 4][:, :, :].rearrange("p a b -> p (a b)")
                    u -= SPLIT * (u >= SPLIT)
                    for ri in range(2):
                        for k in range(tiles):
                            n = u + ri * tiles + k
                            ins = mm(ps[:, 2 * (pos % 4) + ri, :], w[:, n * P:(n + 1) * P], res[:, k0 + k, :],
                                     start=k == 0, stop=k == tiles - 1)
                    ins.then_inc(done, 1)
                    if pos in (4, 7):
                        pe.wait_ge(done, pos + 1)
                        pe.sem_inc(free[(first_chunk + (pos == 7)) % 4], 1)

            def k_wait(pos):
                if pos == 3:
                    pe.wait_ge(mod_ready, 1)
                if pos >= 4:
                    pe.wait_ge(kev, 2 * (pos - 3))
            transforms(RES, 4, kres, k_wait, ku_mm)
            stage_end(pe, 1)

            for g in range(3):
                pe.wait_ge(xn_ready, g + 1)
                width = 4 if g < 2 else CT
                for k in range(DT):
                    n = g * DT + k
                    if n >= 4:
                        pe.wait_ge(tp_act if n % 2 == 0 else tp_dve, (n - 4) // 2 + 1)
                    for j in range(width):
                        ins = nc.tensor.transpose(ps[:, 4 + n % 4, j * P:(j + 1) * P],
                                                  XB[g % 2][:, j, k * P:(k + 1) * P], ID)
                    ins.then_inc(tp_mm, 1)
            stage_end(pe, 2)

            def v_transposes(c):
                pe.wait_ge(v_ready, c + 1)
                for g in range(2):
                    n = 2 * c + g
                    if n >= 4:
                        pe.wait_ge(vt_ev, n - 3)
                    for j in range(4):
                        i = 4 * g + j
                        ins = nc.tensor.transpose(ps[:, 4 + n % 4, j * P:(j + 1) * P], VTMP[c % 2][:, i * P:(i + 1) * P], ID)
                    ins.then_inc(vt_mm, 1)

            for t in range(12):
                chunk = 6 + t // 4
                if t % 4 == 0:
                    arrived(pe, chunk)
                if t >= 2:
                    pe.wait_ge(cv_done, t - 1)
                for h in range(2):
                    for k in range(DT):
                        ins = mm(ps[:, 2 * (t % 2) + h, :], ring[chunk % 4][:, k, (t % 4) * P:(t % 4 + 1) * P],
                                 HT[:, k, h * 512:(h + 1) * 512], start=k == 0, stop=k == DT - 1)
                ins.then_inc(cv_mm, 1)
                if t % 4 == 3:
                    pe.wait_ge(cv_mm, t + 1)
                    pe.sem_inc(free[chunk % 4], 1)
                if t >= 9:
                    v_transposes(t - 9)
            v_transposes(3)
            arrived(pe, 9)
            pe.wait_ge(v_ready, HC)
            for n in range(KT):
                if n < 4:
                    pe.wait_ge(cv_done, 12)
                else:
                    pe.wait_ge(lat_ev, n - 3)
                w, c0 = (HT, 0) if n < TT else (HTC, QR)
                i = n if n < TT else n - TT
                for k in range(DT):
                    ins = mm(ps[:, n % 4, c0:LAT], w[:, k, i * P:(i + 1) * P], ring[9 % 4][:, k, c0:LAT],
                             start=k == 0, stop=k == DT - 1)
                ins.then_inc(lat_mm, 1)
            pe.wait_ge(lat_mm, KT)
            pe.sem_inc(free[9 % 4], 1)
            stage_end(pe, 3)

            def u_wait(pos):
                if pos >= 4:
                    pe.wait_ge(y_prod, pos - 3)
            transforms(RESV, 10, vres, u_wait, u_mm)
            pe.wait_ge(y_prod, 8)
            for j in range(16):
                chunk = 12 + j // 4
                if j % 4 == 0:
                    arrived(pe, chunk)
                w = ring[chunk % 4][:, :, :].rearrange("p a b -> p (a b)")
                for c in range(HC):
                    for h in range(2):
                        ins = mm(ps[:, 2 * c + h, :], SD[:, j, c * P:(c + 1) * P],
                                 w[:, (j % 4) * T + h * 512:(j % 4) * T + (h + 1) * 512], start=j == 0, stop=j == 15)
                        if j == 15 and h == 1:
                            ins.then_inc(inv_mm, 1)
                if j % 4 == 3 and j < 15:
                    ins.then_inc(free[chunk % 4], 1)
            pe.wait_ge(inv_mm, HC)
            pe.sem_inc(free[15 % 4], 1)
            stage_end(pe, 4)

            pe.wait_ge(ln_ready, 1)
            for n in range(7):
                tiles = [range(0, 4), range(4, 8)][n % 2] if n < 4 else [range(0, 4), range(4, 8), range(8, 10)][n - 4]
                c0 = (n // 2) * P if n < 4 else QR
                for j, i in enumerate(tiles):
                    ins = nc.tensor.transpose(ps[:, n, j * P:(j + 1) * P], LATB[:, i, c0:c0 + P], ID)
                ins.then_inc(lt_mm, 1)
            pe.wait_ge(lt_ev, 7)
            pe.wait_ge(att_in, 16 * 4)
            for h in range(NH):
                if h:
                    pe.wait_ge(y_ev, TT * h)
                for b in range(4):
                    for j in range(2):
                        i = 2 * b + j
                        for k in range(2):
                            ins = mm(ps[:, b, j * QK:(j + 1) * QK], CQT[:, k, i * P:(i + 1) * P],
                                     WUQ[:, k, h * QK:(h + 1) * QK], start=k == 0, stop=k == 1)
                    ins.then_inc(q_mm, 1)
                for b in range(5):
                    if b == 4:
                        pe.wait_ge(q_ev, 4 * h + 1)
                    for j in range(2):
                        i = 2 * b + j
                        ins = mm(ps[:, (4 + b) % 8, j * 256:(j + 1) * 256], CKT[:, i * P:(i + 1) * P],
                                 WUKV[:, h * 256:(h + 1) * 256], start=True, stop=True)
                    ins.then_inc(kv_mm, 1)
                pe.wait_ge(q_ev, 4 * h + 4)
                if h == 0:
                    pe.wait_ge(srep_ready, 1)
                    for q in range(2):
                        arrived(pe, 16 + q)
                        for k in range(DT):
                            ins = mm(ps[:, 2 + q, :], SREP[:, k, :], ring[(16 + q) % 4][:, k, :], start=k == 0, stop=k == DT - 1)
                        ins.then_inc(g1_mm, 1)
                        pe.wait_ge(g1_mm, q + 1)
                        pe.sem_inc(free[(16 + q) % 4], 1)
                else:
                    for q in range(2):
                        mod_columns(16 + 2 * h + q, 4 * q, 3, mod2_mm)
                        pe.wait_ge(mod2_mm, 2 * h - 1 + q)
                        pe.sem_inc(free[(16 + 2 * h + q) % 4], 1)
                pe.wait_ge(h_ready, h + 1)
                for g in range(10):
                    if g < 2:
                        src = [(QTK[:, i, 0:NOPE], P) for i in range(4 * g, 4 * g + 4)]
                    elif g < 4:
                        src = [(QRO[:, i, :], ROPE) for i in range(4 * g - 8, 4 * g - 4)]
                    elif g < 7:
                        src = [(KVT[:, i, 0:NOPE], P) for i in range(4 * g - 16, min(4 * g - 12, KT))]
                    else:
                        src = [(KRH[:, i, :], ROPE) for i in range(4 * g - 28, min(4 * g - 24, KT))]
                    if g >= 8:
                        pe.wait_ge(ht_act, 5 * h + g - 7)
                    for j, (t, rows) in enumerate(src):
                        ins = nc.tensor.transpose(ps[0:rows, g % 8, j * P:(j + 1) * P], t, ID)
                    ins.then_inc(ht_mm, 1)
                pe.wait_ge(ht_act, 5 * h + 5)
                pe.wait_ge(ht_dve, 5 * h + 5)

                def scores(i, segs):
                    u = TT * h + i
                    for seg in segs:
                        k0, k1 = 512 * seg, min(512 * (seg + 1), KEYS)
                        o = ps[:, 3 * (u % 2) + seg, 0:k1 - k0]
                        mm(o, QTN[:, i * P:(i + 1) * P], KTN[:, k0:k1], start=True, stop=False)
                        ins = mm(o, QTR[:, i * P:(i + 1) * P], KTR[:, k0:k1], start=False, stop=True)
                        if seg == 2:
                            ins.then_inc(s_mm, 1)

                def turn_p(i, g):
                    u = TT * h + i
                    if g == 0:
                        pe.wait_ge(p_norm, u + 1)
                        if u:
                            pe.wait_ge(pt_act, 2 * u)
                    if g == 1 and u:
                        pe.wait_ge(y_ev, u)
                    if g == 2:
                        pe.wait_ge(pt_act, 2 * u + 1)
                    for j in range(4 if g < 2 else 2):
                        kt = 4 * g + j
                        ins = nc.tensor.transpose(ps[:, 6 + g % 2, j * P:(j + 1) * P], PB[u % 2][:, kt * P:(kt + 1) * P], ID)
                    ins.then_inc(pt_mm, 1)

                def values(i):
                    u = TT * h + i
                    pe.wait_ge(pt_dve, u + 1)
                    for kt in range(KT):
                        if kt == 8:
                            pe.wait_ge(pt_act, 2 * u + 2)
                        ins = mm(ps[:, 7, 0:P], KVT[:, kt, NOPE:], PT[:, kt, :], start=kt == 0, stop=kt == KT - 1)
                    ins.then_inc(o_mm, 1)

                scores(0, (0, 1, 2))
                scores(1, (0, 1, 2))
                for i in range(TT):
                    turn_p(i, 0)
                    turn_p(i, 1)
                    if i + 2 < TT:
                        scores(i + 2, (0, 1))
                    turn_p(i, 2)
                    if i + 2 < TT:
                        scores(i + 2, (2,))
                    values(i)
            stage_end(pe, 5)

            arrived(pe, 24)
            arrived(pe, 25)
            pe.wait_ge(f_in, 16)

            def project(i, h):
                if i >= 2 and h == 0:
                    pe.wait_ge(xnew_ready, i - 1)
                for k in range(DT):
                    lhs = X0T[:, k, i * P:(i + 1) * P] if k < HC else YA[:, k - HC, i * P:(i + 1) * P]
                    ins = mm(ps[:, 2 * (i % 2) + h, :], lhs, ring[(24 + h) % 4][:, k, :], start=k == 0, stop=k == DT - 1)
                if h == 1:
                    ins.then_inc(wo_mm, 1)

            def turn(i):
                pe.wait_ge(fxn, i + 1)
                for g in range(2):
                    if i:
                        pe.wait_ge(ft_act if g == 0 else ft_dve, i)
                    for j in range(4):
                        k = 4 * g + j
                        ins = nc.tensor.transpose(ps[:, 4 + g, j * P:(j + 1) * P], XNB[i % 2][:, k * P:(k + 1) * P], ID)
                    ins.then_inc(ft_mm, 1)

            def logits(i):
                pe.wait_ge(ft_act, i + 1)
                pe.wait_ge(ft_dve, i + 1)
                for k in range(DT):
                    ins = mm(ps[:, 6, 0:NE], H2T[i % 2][:, k, :], RW[:, k, :], start=k == 0, stop=k == DT - 1)
                ins.then_inc(lg_mm, 1)

            def rank(i):
                pe.wait_ge(route_m, i + 1)
                mm(ps[:, 7, 0:NE], TRI, RTW[:, NE:2 * NE], start=True, stop=False)
                mm(ps[:, 7, 0:NE], ONE, RTW[:, 2 * NE:3 * NE], start=False, stop=True).then_inc(rk_mm, 1)

            for i in range(TT + 2):
                if i < TT:
                    project(i, 0)
                if 1 <= i <= TT:
                    turn(i - 1)
                if i >= 2:
                    rank(i - 2)
                if i < TT:
                    project(i, 1)
                if 1 <= i <= TT:
                    logits(i - 1)
                if i == TT:
                    pe.wait_ge(wo_mm, TT)
                    pe.sem_inc(free[0], 1)
                    pe.sem_inc(free[1], 1)
            pe.wait_ge(slot_ready, TT)
            mm(ps[:, 7, 0:NE], ONE, RTW[:, 2 * NE:3 * NE], start=True, stop=True).then_inc(cnt_mm, 1)
            pe.wait_ge(list_in, 32)
            for g in range(2):
                for o in range(2):
                    ins = nc.tensor.transpose(ps[:, 6, (2 * o + g) * P:(2 * o + g + 1) * P], JF[:, 2 * P * g + o:2 * P * (g + 1):2], ID)
            ins.then_inc(list_mm, 1)
            stage_end(pe, 6)

            pe.wait_ge(cnt_ready, 1)
            for slot in (4, 5):
                pe.sem_inc(free[slot], 1)
            def turn_rows(g, base, count):
                pe.wait_ge(rows_ready, g + 1)

                def body(w):
                    nb = w // P
                    n = max(1, NB // nb) if nb != 3 else 1
                    for group in range(DT // n):
                        pe.wait_ge(tp_evac, base + 2 + max(0, group - 1) * n)
                        for k in range(group * n, (group + 1) * n):
                            for b in range(nb):
                                at_ = (k % n) * w + b * P
                                ins = nc.tensor.transpose(ps[:, 6 + group % 2, at_:at_ + P], XSR[:, b, k * P:(k + 1) * P], ID)
                        ins.then_inc(tp_done, n)
                by_width(pe, count, BLOCKS, body)

            def one(it, e, block, count, count_next):
                if block:
                    turn_rows(it + 1, it * 16 + 8, count)
                    pe.wait_ge(tp_evac, it * 16 + 18)
                else:
                    pe.wait_ge(tp_evac, it * 16 + 2)

                def gate_up(w):
                    for c in range(4):
                        pe.wait_ge(full[WSLOT[c]], (it + 1 + USES[WSLOT[c]]) * 16)
                        for m in range(4):
                            t = 4 * c + m
                            pe.wait_ge(gu_evac, it * 16 + t + 1)
                            for k in range(DT):
                                ins = mm(ps[:, m, 0:w], ring[WSLOT[c]][:, k, m * P:(m + 1) * P], XST[:, k, 0:w],
                                         start=k == 0, stop=k == DT - 1)
                                if m == 0 and k == 0 and c:
                                    ins.then_inc(free[WSLOT[c - 1]], 1)
                            ins.then_inc(gu_done, 1)
                by_width(pe, count, WIDTHS, gate_up)
                if not block:
                    turn_rows(it + 1, it * 16 + 8, count_next)

                def down(w):
                    for c in range(2):
                        pe.wait_ge(full[4 + c], (it + 1) * 16)
                        for m in range(4):
                            d = 4 * c + m
                            pe.wait_ge(yt_ready, it * 8 + d + 1)
                            for k in range(DT):
                                if d == 0:
                                    pe.wait_ge(he_ready, it * 8 + k + 1)
                                ins = mm(ps[:, 4 + d % 2, 0:w], ring[4 + c][:, k, m * P:(m + 1) * P], HE[:, k, 0:w],
                                         start=k == 0, stop=k == DT - 1)
                                if m == 0 and k == 0:
                                    ins.then_inc(free[WSLOT[3 + c]], 1)
                            ins.then_inc(y_done, 1)
                    nb = (w + P - 1) // P
                    for g in range(2 * nb):
                        pe.wait_ge(tp_evac, it * 16 + 16 + g + 1)
                        for j in range(4):
                            k = 4 * (g % 2) + j
                            if g < 2:
                                pe.wait_ge(yt_ready, it * 8 + k + 3)
                            ins = nc.tensor.transpose(ps[:, 6 + g % 2, j * P:(j + 1) * P],
                                                      YT[:, k, (g // 2) * P:(g // 2 + 1) * P], ID)
                            if g == 0 and j == 0:
                                ins.then_inc(free[5], 1)
                        ins.then_inc(tp_done, 1 if g < 2 * nb - 1 else 1 + 2 * (NB - nb))
                by_width(pe, count, WIDTHS, down)

            turn_rows(0, 0, pe.value_load(CNT[0:1, 0:1], min_val=0, max_val=CAP))
            pe.wait_ge(tp_evac, 10)
            passes(pe, one)
            stage_end(pe, 7)

        @block.scalar
        def _(act):
            n_step = [0]

            def step(ins):
                n_step[0] += 1
                ins.then_inc(act_step, 1)
                act.wait_ge(act_step, n_step[0])

            made = {}

            def give(ins, ready):
                made[ready] = made.get(ready, 0) + 1
                ins.then_inc(ready, 1)
                act.wait_ge(ready, made[ready])

            fn = nc.scalar.activation
            act.dma_start(PAR[:, :], a["par"]).then_inc(c_in, 16)
            act.dma_start(ZS[:, :], a["k_z"]).then_inc(filt_in, 16)
            act.dma_start(FW[:, :], a["fw"]).then_inc(filt_in, 16)
            act.dma_start(SM[:, :], a["k_small"]).then_inc(filt_in, 16)
            act.dma_start(DEC[:, :, :, :].rearrange("p t r c -> p (t r c)"),
                          a["k_decay"].rearrange("p t r c -> p (t r c)")).then_inc(par_in, 16)
            act.dma_start(BIAS[0:1, :], a["hy_bias"]).then_inc(par_in, 16)
            act.dma_start(BGU[:, :], a["b_gu"]).then_inc(par_in, 16)
            act.dma_start(BDN[:, :], a["b_dn"]).then_inc(par_in, 16)
            act.dma_start(ROWS[:, :], a["rows"][:, D:]).then_inc(par_in, 16)
            act.wait_ge(c_in, 16)
            give(fn(SIL[:, :], PAR[:, COLS["c"]:COLS["c"] + 16], ACT.Sigmoid), sil_in)
            for l in range(3):
                act.wait_ge(mlp_arg, l + 1)
                give(fn((HA, HB, HA)[l][:, :], (HB, HA, HB)[l][:, :], ACT.Sin), mlp_sin)
            x_v = a["x"].rearrange("(i p) d -> p i d", p=P)
            c_v = a["ctx"].rearrange("(i p) d -> p i d", p=P)
            for i in range(TT):
                act.wait_ge(ab_ready, i + 1)
                if i >= 2:
                    act.wait_ge(norm_mm, i - 1)
                give(fn(ABS[i % 2][:, :, :].rearrange("p r c -> p (r c)"), AB[i % 2][:, :, :].rearrange("p r c -> p (r c)"),
                        ACT.Abs), abs_done)
            act.wait_ge(fk_done, TT)
            for g in range(2):
                act.dma_start(XB[g][:, :, :], x_v[:, 4 * g:4 * g + 4, :]).then_inc(x_in[g], 16)

            def squares(g):
                act.wait_ge(x_in[g], 16)
                for j in range(4 if g < 2 else CT):
                    n = 4 * g + j
                    step(fn(JUNK[:, :], XB[g % 2][:, j, :], ACT.Square, accum_out=ST[:, n:n + 1]))
                act.nop().then_inc(ssq_ready, 1)

            def root(ready, lo, hi, done, n):
                act.wait_ge(ready, n)
                give(fn(ST[:, lo:hi], ST[:, lo:hi], ACT.Sqrt), done)

            squares(0)
            root(var_ready, 10, 14, std_ready, 1)
            squares(1)
            root(var_ready, 14, 18, std_ready, 2)
            act.wait_ge(kres, 2)
            for pos, pair in enumerate(ORDER):
                act.wait_ge(ku_mm, pos + 1)
                for ri in range(2):
                    give(fn(SD[:, 2 * pair + ri, :], ps[:, 2 * (pos % 4) + ri, :], ACT.Copy), kev)
            stage_end(act, 1)
            def fill(g):
                for k in range(0, DT, 2):
                    act.wait_ge(tp_mm, g * DT + k + 1)
                    dst, s = (HT[:, k, g * 512:(g + 1) * 512], 0) if g < 2 else (HTC[:, k, :], 1)
                    w = 512 if g < 2 else CTX
                    give(fn(dst, ps[:, 4 + (g * DT + k) % 4, 0:w], ACT.Identity, scale=A1[:, k, s:s + 1],
                       bias=MODC[:, 0, k, s:s + 1]), tp_act)

            act.wait_ge(mod_ready, 1)
            fill(0)
            act.wait_ge(tp_mm, DT)
            act.dma_start(XB[0][:, 0:CT, :], c_v).then_inc(x_in[2], 16)
            squares(2)
            root(var_ready, 18, 20, std_ready, 3)
            fill(1)
            fill(2)
            stage_end(act, 2)
            for t in range(12):
                dst = X0T[:, t, :] if t < 4 else X1T[:, t - 4, :] if t < 8 else VTMP[t % 2][:, :]
                if t >= 10:
                    act.wait_ge(vt_mm, 2 * (t - 9))
                act.wait_ge(cv_mm, t + 1)
                w1 = COLS["convw"] + 12 + t
                give(fn(dst, banks(2 * (t % 2)), ACT.Identity, scale=PAR[:, w1:w1 + 1],
                   bias=PAR[:, COLS["convb"] + t:COLS["convb"] + t + 1]), cv_act)
                if t in (10, 11):
                    for g in range(2):
                        n = 2 * (t - 10) + g
                        act.wait_ge(vt_mm, n + 1)
                        give(fn(VTOK[:, 4 * g:4 * g + 4, (t - 10) * P:(t - 9) * P],
                           ps[:, 4 + n % 4, :].rearrange("p (i c) -> p i c", c=P), ACT.Copy), vt_ev)
            for n in range(4, 8):
                act.wait_ge(vt_mm, n + 1)
                give(fn(VTOK[:, 4 * (n % 2):4 * (n % 2) + 4, (n // 2) * P:(n // 2 + 1) * P],
                   ps[:, 4 + n % 4, :].rearrange("p (i c) -> p i c", c=P), ACT.Copy), vt_ev)
            for n in range(KT):
                act.wait_ge(lat_mm, n + 1)
                c0 = 0 if n < TT else QR
                give(fn(LATB[:, n, c0:LAT], ps[:, n % 4, c0:LAT], ACT.Copy), lat_ev)
            stage_end(act, 3)
            for n in range(KT):
                if n < TT:
                    step(fn(JE[:, 0:QR], LATB[:, n, 0:QR], ACT.Square, accum_out=ST[:, 20 + n:21 + n]))
                step(fn(JE[:, 0:KR], LATB[:, n, QR:QR + KR], ACT.Square, accum_out=ST[:, 28 + n:29 + n]))
                step(fn(JE[:, 0:ROPE], LATB[:, n, QR + KR:], ACT.Square, accum_out=ST[:, 38 + n:39 + n]))
            act.nop().then_inc(lss, 1)
            root(lvar, 48, 66, lstd, 1)
            stage_end(act, 4)
            act.dma_start(WUQ[:, :, :], a["w_uq"].rearrange("(k p) n -> p k n", p=P)).then_inc(att_in, 16)
            act.dma_start(WUKV[:, :], a["w_ukv"]).then_inc(att_in, 16)
            act.dma_start(G1B[:, :], a["rows"][:, 0:D]).then_inc(att_in, 16)
            act.dma_start(ROPT[:, :, :, :].rearrange("p s t f -> p (s t f)"),
                          a["k_rope"].rearrange("p s t f -> p (s t f)")).then_inc(att_in, 16)
            for n in range(7):
                act.wait_ge(lt_mm, n + 1)
                if n < 4:
                    c = COLS["qn"] + n // 2
                    give(fn(CQT[:, n // 2, (n % 2) * 512:(n % 2 + 1) * 512], ps[:, n, :], ACT.Copy,
                       scale=PAR[:, c:c + 1]), lt_ev)
                else:
                    g = n - 4
                    w = 512 if g < 2 else 256
                    give(fn(CKT[:, g * 512:g * 512 + w], ps[:, n, 0:w], ACT.Copy,
                       scale=PAR[:, COLS["kvn"]:COLS["kvn"] + 1]), lt_ev)
            for h in range(NH):
                for b in range(4):
                    act.wait_ge(q_mm, 4 * h + b + 1)
                    give(fn(QTK[:, 2 * b:2 * b + 2, :].rearrange("p t c -> p (t c)"), ps[:, b, 0:2 * QK],
                       ACT.Copy), q_ev)
                act.wait_ge(q_ev, 4 * h + 4)
                for i in range(TT):
                    step(fn(JE[:, 0:QK], QTK[:, i, :], ACT.Square, accum_out=ST[:, 66 + i:67 + i]))
                act.wait_ge(kv_ev, 5 * h + 5)
                for i in range(KT):
                    step(fn(JE[:, 0:NOPE], KVT[:, i, 0:NOPE], ACT.Square, accum_out=ST[:, 74 + i:75 + i]))
                act.nop().then_inc(hss, 1)
                root(hvar, 84, 102, hstd, h + 1)
                for g in (0, 1, 4, 5, 6):
                    act.wait_ge(ht_mm, 10 * h + g + 1)
                    if g < 2:
                        give(fn(QTN[:, g * 512:(g + 1) * 512], ps[:, g, :], ACT.Copy, scale=FB[:, 3:4]), ht_act)
                    else:
                        w = 512 if g < 6 else 256
                        give(fn(KTN[:, (g - 4) * 512:(g - 4) * 512 + w], ps[:, g, 0:w], ACT.Copy), ht_act)

                def softmax(i):
                    u = TT * h + i
                    act.wait_ge(s_max, u + 1)
                    if u >= 2:
                        act.wait_ge(pt_mm, 3 * (u - 1))
                    b = 3 * (u % 2)
                    give(fn(PB[u % 2][:, :], banks(b, 3)[:, 0:KEYS], ACT.Exp, bias=ST[:, 104 + u % 2:105 + u % 2],
                       accum_out=ST[:, 106 + u % 2:107 + u % 2]), p_ready)

                def pt_store(i, g):
                    u = TT * h + i
                    act.wait_ge(pt_mm, 3 * u + g + 1)
                    w = 4 if g < 2 else 2
                    give(fn(PT[:, 4 * g:4 * g + w, :].rearrange("p a b -> p (a b)"), ps[:, 6, 0:w * P],
                       ACT.Copy), pt_act)

                softmax(0)
                for i in range(TT):
                    pt_store(i, 0)
                    if i + 1 < TT:
                        softmax(i + 1)
                    pt_store(i, 2)
                    act.wait_ge(o_mm, TT * h + i + 1)
                    give(fn(YA[:, h, i * P:(i + 1) * P], ps[:, 7, 0:P], ACT.Copy), y_ev)
            stage_end(act, 5)
            act.dma_start(RW[:, :, :], a["router_w"].rearrange("(k p) e -> p k e", p=P)).then_inc(f_in, 16)
            for i in range(2):
                act.dma_start(XIN[i][:, :], a["x"][i * P:(i + 1) * P, :]).then_inc(xo_in[i], 16)
            for i in range(TT + 1):
                if i:
                    t = i - 1
                    act.wait_ge(ft_mm, 2 * t + 1)
                    act.dma_start(xn_d[t * P:(t + 1) * P, :], XNB[t % 2][:, :]).then_inc(xn_out[t % 2], 16)
                    act.dma_start(out[t * P:(t + 1) * P, :], XNEW[:, t % 2, :]).then_inc(xnew_out[t % 2], 16)
                    for j in range(4):
                        ins = fn(H2T[t % 2][:, j, :], ps[:, 4, j * P:(j + 1) * P], ACT.Identity, scale=A2[:, j:j + 1],
                                 bias=MODC[:, 2, j, 0:1])
                    give(ins, ft_act)
                if i < TT:
                    act.wait_ge(xnew_ready, i + 1)
                    step(fn(JF[:, :], XNEW[:, i % 2, :], ACT.Square, accum_out=ST[:, i:i + 1]))
                    act.nop().then_inc(fss, 1)
                    if i + 2 < TT:
                        act.dma_start(XIN[i % 2][:, :], a["x"][(i + 2) * P:(i + 3) * P, :]).then_inc(xo_in[i % 2], 16)
                    root(fvar, 10 + i, 11 + i, fstd, i + 1)
                if i:
                    act.wait_ge(gneg, i)
                    give(fn(RTW[:, 8 * NE + 16:8 * NE + 20], RTW[:, 8 * NE:8 * NE + 4], ACT.Exp, bias=RTW[:, 8 * NE + 24:8 * NE + 25],
                            accum_out=RTW[:, 8 * NE + 25:8 * NE + 26]), gexp)
            for i in range(2):
                act.wait_ge(xn_out[i], 16 * (TT // 2))
                act.wait_ge(xnew_out[i], 16 * (TT // 2))
            stage_end(act, 6)

            act.wait_ge(cnt_ready, 1)
            act.sem_inc(tp_evac, 2)

            def store_rows(base, count):
                def body(w):
                    nb = w // P
                    n = max(1, NB // nb) if nb != 3 else 1
                    for k in range(DT):
                        if k % n == 0:
                            act.wait_ge(tp_done, base + k + n)
                        fn(XST[:, k, 0:w], ps[:, 6 + k // n % 2, (k % n) * w:(k % n + 1) * w], ACT.Identity, scale=A2[:, k:k + 1],
                           bias=MODC[:, 2, k, 0:1]).then_inc(tp_evac, 1)
                by_width(act, count, BLOCKS, body)

            def one(it, e, block, count, count_next):
                if block:
                    store_rows(it * 16 + 8, count)

                def sigmoids(w):
                    for m in range(DT):
                        act.wait_ge(gu_evac, it * 16 + 4 + 8 * (m // 4) + m % 4 + 1)
                        fn(SG[:, m % 2, 0:w], GA[:, m % 2, 0:w], ACT.Sigmoid, scale=ALPHA).then_inc(sg_ready, 1)
                by_width(act, count, BLOCKS, sigmoids)
                if not block:
                    store_rows(it * 16 + 8, count_next)

                def results(w):
                    act.wait_ge(gates_ready, it + 1)
                    act.wait_ge(yr_free, it + 1)
                    nb = w // P
                    for g in range(2 * nb):
                        act.wait_ge(tp_done, it * 16 + 16 + g + 1)
                        fn(YR[:, g // 2, (g % 2) * 512:(g % 2 + 1) * 512], ps[:, 6 + g % 2, :],
                           ACT.Copy, scale=GATES[:, g // 2:g // 2 + 1]).then_inc(tp_evac, 1 if g < 2 * nb - 1 else 1 + 2 * (NB - nb))
                by_width(act, count, BLOCKS, results)

            store_rows(0, act.value_load(CNT[0:1, 0:1], min_val=0, max_val=CAP))
            passes(act, one)
            stage_end(act, 7)

        @block.vector
        def _(dve):
            n_step = [0]
            v = nc.vector

            def step(ins):
                n_step[0] += 1
                ins.then_inc(dve_step, 1)
                dve.wait_ge(dve_step, n_step[0])

            made = {}

            def give(ins, ready):
                made[ready] = made.get(ready, 0) + 1
                ins.then_inc(ready, 1)
                dve.wait_ge(ready, made[ready])

            tt, ts, stt = v.tensor_tensor, v.tensor_scalar, v.scalar_tensor_tensor
            dve.wait_ge(c_in, 16)
            dve.wait_ge(sil_in, 1)
            give(tt(SIL[:, :], SIL[:, :], PAR[:, COLS["c"]:COLS["c"] + 16], ALU.mult), sil_ready)
            fc = PAR[:, COLS["freq"]:COLS["freq"] + 1]
            for l in range(3):
                b = COLS["b1"] + l
                step(tt(FB[:, l:l + 1], PAR[:, b:b + 1], fc, ALU.mult))
            step(tt(FB[:, 3:4], PAR[:, COLS["gq"]:COLS["gq"] + 1], PAR[:, COLS["gk"]:COLS["gk"] + 1], ALU.mult))
            step(ts(FB[:, 3:4], FB[:, 3:4], SCALE, None, ALU.mult))
            c1 = 6.28125
            c2 = 2.0 ** -24 * round((2 * math.pi - c1) * 2.0 ** 24 / 4096) * 4096
            c3 = 2 * math.pi - c1 - c2
            for l in range(3):
                dst = (HB, HA, HB)[l]
                dve.wait_ge(mlp_mm, 2 * l + 2)
                step(ts(dst[:, :], banks(0), fc, FB[:, l:l + 1], ALU.mult, ALU.add))
                step(ts(RN[:, :], dst[:, :], 1 / (2 * math.pi), MAGIC, ALU.mult, ALU.add))
                step(ts(RN[:, :], RN[:, :], MAGIC, None, ALU.subtract))
                for c in (c1, c2, c3):
                    step(stt(out=dst[:, :], in0=RN[:, :], scalar=-c, in1=dst[:, :], op0=ALU.mult, op1=ALU.add))
                give(ts(dst[:, :], dst[:, :], 3.1415925, -3.1415925, ALU.min, ALU.max), mlp_arg)
            dve.wait_ge(par_in, 16 * 5)
            for i in range(TT):
                dve.wait_ge(fk_mm, i + 1)
                if i >= 2:
                    dve.wait_ge(abs_done, i - 1)
                b = 2 * (i % 2)
                ab = AB[i % 2]
                give(tt(ab[:, :, :].rearrange("p r c -> p (r c)"), banks(b), DEC[:, i, :, :].rearrange("p r c -> p (r c)"), ALU.mult), ab_ready)
                if i == 0:
                    dve.wait_ge(abs_done, 1)
                    step(v.memset(ab[0:1, 1, :], 0.0))
                tt(SD[:, i, :], ab[:, 0, :], ab[:, 1, :], ALU.add)
                give(tt(SD[:, 8 + i, :], ab[:, 0, :], ab[:, 1, :], ALU.subtract), fk_done)
            dve.wait_ge(norm_mm, TT)
            give(v.tensor_copy(RN[0:1, HY:2 * HY], ps[0:1, 4, :]), norm_row)
            step(tt(RN[0:1, 0:HY], BIAS[0:1, :], RN[0:1, HY:2 * HY], ALU.mult))
            dve.wait_ge(norm_col, 1)
            step(v.reciprocal(RNC[:, :], ps[:, 5, 0:HC]))
            step(tt(SD[0:1, 0, :], SD[0:1, 0, :], RN[0:1, 0:HY], ALU.add))
            step(tt(SD[0:1, 8, :], SD[0:1, 8, :], RN[0:1, 0:HY], ALU.add))

            def residues(cyc, neg, res, tmp, done):
                s2 = math.sqrt(2.0)
                step(tt(tmp[:, :, :], cyc[:, 0:4, :], cyc[:, 4:8, :], ALU.add))
                step(tt(res[:, 8:12, :], cyc[:, 0:4, :], cyc[:, 4:8, :], ALU.subtract))
                step(tt(res[:, 12:14, :], tmp[:, 0:2, :], tmp[:, 2:4, :], ALU.subtract))
                give(tt(res[:, 14:16, :], tmp[:, 0:2, :], tmp[:, 2:4, :], ALU.add), done)
                step(tt(tmp[:, 0:2, :], neg[:, 0:2, :], neg[:, 4:6, :], ALU.subtract))
                step(tt(tmp[:, 2:4, :], neg[:, 2:4, :], neg[:, 6:8, :], ALU.add))
                for r, s in ((0, s2), (4, -s2)):
                    step(stt(out=res[:, r:r + 2, :], in0=neg[:, 6:8, :], scalar=s, in1=tmp[:, 0:2, :], op0=ALU.mult, op1=ALU.add))
                    ins = stt(out=res[:, r + 2:r + 4, :], in0=neg[:, 4:6, :], scalar=-s, in1=tmp[:, 2:4, :], op0=ALU.mult, op1=ALU.add)
                    if r == 0:
                        step(ins)
                give(ins, done)

            residues(SD[:, 0:8, :], SD[:, 8:16, :], RES, TMP, kres)
            mb = COLS["modb"]
            dve.wait_ge(mod_mm, 4)
            for s in range(2):
                src = ps[:, 7, 0:32].rearrange("p (m k s) -> p m k s", m=2, s=2)
                step(tt(MODC[:, 0:2, :, s], src[:, :, :, s], PAR[:, mb:mb + 16].rearrange("p (m k) -> p m k", m=2), ALU.add))
                ins = stt(out=A1[:, :, s], in0=MODC[:, 1, :, s], scalar=1.0, in1=PAR[:, COLS["norm1"]:COLS["norm1"] + 8],
                          op0=ALU.add, op1=ALU.mult)
                if s == 0:
                    step(ins)
            give(ins, mod_ready)
            dve.wait_ge(mod_ready, 1)
            def inverse_std(lo, n, scale, ready, std, k, off):
                give(ts(ST[:, lo + off:lo + off + n], ST[:, lo:lo + n], scale, EPS, ALU.mult, ALU.add), ready)
                dve.wait_ge(std, k)
                step(v.reciprocal(ST[:, lo + off:lo + off + n], ST[:, lo + off:lo + off + n]))

            def scale_x(g):
                n = 4 if g < 2 else CT
                dve.wait_ge(ssq_ready, g + 1)
                inverse_std(4 * g, n, 1.0 / D, var_ready, std_ready, g + 1, 10)
                for j in range(n):
                    ins = ts(XB[g % 2][:, j, :], XB[g % 2][:, j, :], ST[:, 10 + 4 * g + j:11 + 4 * g + j], None, ALU.mult)
                give(ins, xn_ready)

            scale_x(0)
            scale_x(1)
            stage_end(dve, 1)

            def fill(g):
                for k in range(1, DT, 2):
                    dve.wait_ge(tp_mm, g * DT + k + 1)
                    dst, s = (HT[:, k, g * 512:(g + 1) * 512], 0) if g < 2 else (HTC[:, k, :], 1)
                    w = 512 if g < 2 else CTX
                    give(ts(dst, ps[:, 4 + (g * DT + k) % 4, 0:w], A1[:, k, s:s + 1], MODC[:, 0, k, s:s + 1],
                       ALU.mult, ALU.add), tp_dve)

            fill(0)
            scale_x(2)
            fill(1)
            fill(2)
            stage_end(dve, 2)

            for t in range(12):
                dst = X0T[:, t, :] if t < 4 else X1T[:, t - 4, :] if t < 8 else VTMP[t % 2][:, :]
                dve.wait_ge(cv_act, t + 1)
                w = COLS["convw"] + t
                u = banks(2 * (t % 2))
                step(stt(out=dst[:, 1:T], in0=u[:, 0:T - 1], scalar=PAR[:, w:w + 1], in1=dst[:, 1:T], op0=ALU.mult, op1=ALU.add))
                give(stt(out=dst[:, 0:T - 1], in0=u[:, 1:T], scalar=PAR[:, w + 24:w + 25], in1=dst[:, 0:T - 1],
                    op0=ALU.mult, op1=ALU.add), cv_done)
                if t < 4 or t >= 8:
                    dve.wait_ge(cv_done, t + 1)
                if t < 4:
                    ts(dst, dst, RNC[:, t:t + 1], None, ALU.mult)
                if t >= 8:
                    give(tt(dst, dst, X1T[:, t - 8, :], ALU.mult), v_ready)
            stage_end(dve, 3)

            residues(VTOK[:, :, :], VTOK[:, :, :], RESV, TMPV, vres)
            for pos, pair in enumerate(ORDER):
                dve.wait_ge(u_mm, pos + 1)
                b = 2 * (pos % 4)
                kr, ki = SD[:, 2 * pair, :], SD[:, 2 * pair + 1, :]
                tt(PR[:, 0, :], ps[:, b, :], kr, ALU.mult)
                tt(PR[:, 1, :], ps[:, b + 1, :], ki, ALU.mult)
                tt(PR[:, 2, :], ps[:, b, :], ki, ALU.mult)
                step(tt(PR[:, 3, :], ps[:, b + 1, :], kr, ALU.mult))
                tt(kr, PR[:, 0, :], PR[:, 1, :], ALU.subtract)
                ins = tt(ki, PR[:, 2, :], PR[:, 3, :], ALU.add)
                if pair == 7:
                    step(ins)
                    v.tensor_copy(kr[0:1, :], PR[0:1, 0, :])
                    ins = v.tensor_copy(ki[0:1, :], PR[0:1, 1, :])
                give(ins, y_prod)
                dve.wait_ge(y_prod, pos + 1)
            dve.wait_ge(lss, 1)
            ts(ST[:, 48:56], ST[:, 20:28], 1.0 / QR, EPS, ALU.mult, ALU.add)
            give(ts(ST[:, 56:66], ST[:, 28:38], 1.0 / KR, EPS, ALU.mult, ALU.add), lvar)
            dve.wait_ge(lstd, 1)
            step(v.reciprocal(ST[:, 48:66], ST[:, 48:66]))
            for n in range(KT):
                if n < TT:
                    ts(LATB[:, n, 0:QR], LATB[:, n, 0:QR], ST[:, 48 + n:49 + n], None, ALU.mult)
                ins = ts(LATB[:, n, QR:QR + KR], LATB[:, n, QR:QR + KR], ST[:, 56 + n:57 + n], None, ALU.mult)
            give(ins, ln_ready)
            for c in range(HC):
                dve.wait_ge(inv_mm, c + 1)
                tt(X0T[:, c, :], X0T[:, c, :], banks(2 * c), ALU.mult)
            stage_end(dve, 4)

            for k in range(DT):
                ins = ts(SREP[:, k, :], ONE, SIL[:, k:k + 1], None, ALU.mult)
            give(ins, srep_ready)
            for n in range(KT):
                ins = tt(KRT[:, n, :], LATB[:, n, QR + KR:], ROWS[:, NE + ROPE:NE + 2 * ROPE], ALU.mult)
            step(ins)
            dve.wait_ge(att_in, 16 * 4)

            def rotate(x):
                x = x.rearrange("p t (a b f) -> p t a b f", a=2, b=2)
                cs = [ROPT[:, s, :, :].rearrange("p t (a f) -> p t a f", a=2) for s in range(2)]
                r = [RT[:, s, :, :].rearrange("p t (a f) -> p t a f", a=2) for s in range(2)]
                for a_ in range(2):
                    x1, x2 = x[:, :, a_, 0, :], x[:, :, a_, 1, :]
                    c, s = cs[0][:, :, a_, :], cs[1][:, :, a_, :]
                    r0, r1 = r[0][:, :, a_, :], r[1][:, :, a_, :]
                    tt(r0, x2, s, ALU.mult)
                    step(tt(r1, x1, s, ALU.mult))
                    tt(x1, x1, c, ALU.mult)
                    step(tt(x2, x2, c, ALU.mult))
                    tt(x1, x1, r0, ALU.subtract)
                    step(tt(x2, x2, r1, ALU.add))

            rotate(KRT[:, 0:TT, :])
            for h in range(NH):
                for b in range(5):
                    dve.wait_ge(kv_mm, 5 * h + b + 1)
                    give(v.tensor_copy(KVT[:, 2 * b:2 * b + 2, :].rearrange("p t c -> p (t c)"), ps[:, (4 + b) % 8, :]), kv_ev)
                dve.wait_ge(hss, h + 1)
                step(tt(ST[:, 74:84], ST[:, 74:84], ST[:, 38:48], ALU.add))
                give(ts(ST[:, 84:102], ST[:, 66:84], 1.0 / QK, EPS, ALU.mult, ALU.add), hvar)
                dve.wait_ge(hstd, h + 1)
                step(v.reciprocal(ST[:, 84:102], ST[:, 84:102]))
                for i in range(TT):
                    ts(QTK[:, i, 0:NOPE], QTK[:, i, 0:NOPE], ST[:, 84 + i:85 + i], None, ALU.mult)
                    ins = stt(out=QRO[:, i, :], in0=QTK[:, i, NOPE:], scalar=ST[:, 84 + i:85 + i], in1=ROWS[:, NE:NE + ROPE],
                              op0=ALU.mult, op1=ALU.mult)
                for i in range(KT):
                    ts(KVT[:, i, 0:NOPE], KVT[:, i, 0:NOPE], ST[:, 92 + i:93 + i], None, ALU.mult)
                    ins = ts(KRH[:, i, :], KRT[:, i, :], ST[:, 92 + i:93 + i], None, ALU.mult)
                step(ins)
                rotate(QRO[:, :, :])
                if h == 0:
                    dve.wait_ge(g1_mm, 2)
                    step(tt(G1B[:, :], banks(2), G1B[:, :], ALU.add))
                else:
                    dve.wait_ge(mod2_mm, 2 * h)
                    b = mb + 24 + 8 * (h - 1)
                    step(tt(MODC[:, 1 + h, :, 0], ps[:, 3, 0:16].rearrange("p (k s) -> p k s", s=2)[:, :, 0], PAR[:, b:b + 8], ALU.add))
                if h == 2:
                    step(stt(out=A2[:, :], in0=MODC[:, 3, :, 0], scalar=1.0, in1=PAR[:, COLS["norm2"]:COLS["norm2"] + 8],
                             op0=ALU.add, op1=ALU.mult))
                give(v.memset(ST[:, 103:104], 0.0), h_ready)
                for g in (2, 3, 7, 8, 9):
                    dve.wait_ge(ht_mm, 10 * h + g + 1)
                    if g < 4:
                        give(ts(QTR[:, (g - 2) * 512:(g - 1) * 512], ps[0:64, g, :], SCALE, None, ALU.mult), ht_dve)
                    else:
                        w = 512 if g < 9 else 256
                        give(v.tensor_copy(KTR[:, (g - 7) * 512:(g - 7) * 512 + w], ps[0:64, g % 8, 0:w]), ht_dve)

                def most_score(i):
                    u = TT * h + i
                    dve.wait_ge(s_mm, u + 1)
                    step(v.tensor_reduce(ST[:, 108 + u % 2:109 + u % 2], banks(3 * (u % 2), 3)[:, 0:KEYS], X, ALU.max))
                    give(ts(ST[:, 104 + u % 2:105 + u % 2], ST[:, 108 + u % 2:109 + u % 2], -1.0, None, ALU.mult), s_max)

                def normalise(i):
                    u = TT * h + i
                    dve.wait_ge(p_ready, u + 1)
                    step(v.reciprocal(ST[:, 110:111], ST[:, 106 + u % 2:107 + u % 2]))
                    give(ts(PB[u % 2][:, :], PB[u % 2][:, :], ST[:, 110:111], None, ALU.mult), p_norm)

                most_score(0)
                most_score(1)
                normalise(0)
                for i in range(TT):
                    dve.wait_ge(pt_mm, 3 * (TT * h + i) + 2)
                    give(v.tensor_copy(PT[:, 4:8, :].rearrange("p a b -> p (a b)"), ps[:, 7, :]), pt_dve)
                    if i + 1 < TT:
                        normalise(i + 1)
                    if i + 2 < TT:
                        most_score(i + 2)
            stage_end(dve, 5)

            step(v.memset(RTW[:, 2 * NE:3 * NE], 0.0))
            up_bias = BGU[:, :].rearrange("p (e r) -> p e r", r=16)[:, :, 8:16]
            ts(up_bias, up_bias, 1.0, None, ALU.add)
            v.tensor_copy(PAIR[:, :, 0], TOKENS)
            step(v.memset(LTOK[:, NE * LCOL:].bitcast(F32), 0.0))
            W = lambda n, w=1: RTW[:, 8 * NE + n:8 * NE + n + w]

            def residual(i):
                dve.wait_ge(wo_mm, i + 1)
                dve.wait_ge(xo_in[i % 2], 16 * (i // 2 + 1))
                if i >= 2:
                    dve.wait_ge(xnew_out[i % 2], 16 * (i // 2))
                step(tt(XNEW[:, i % 2, :], banks(2 * (i % 2)), G1B[:, :], ALU.mult))
                give(tt(XNEW[:, i % 2, :], XNEW[:, i % 2, :], XIN[i % 2][:, :], ALU.add), xnew_ready)
                dve.wait_ge(fss, i + 1)
                give(ts(ST[:, 10 + i:11 + i], ST[:, i:i + 1], 1.0 / D, EPS, ALU.mult, ALU.add), fvar)
                dve.wait_ge(fstd, i + 1)
                step(v.reciprocal(ST[:, 10 + i:11 + i], ST[:, 10 + i:11 + i]))
                if i >= 2:
                    dve.wait_ge(xn_out[i % 2], 16 * (i // 2))
                give(ts(XNB[i % 2][:, :], XNEW[:, i % 2, :], ST[:, 10 + i:11 + i], None, ALU.mult), fxn)

            def fill_h2(i):
                dve.wait_ge(ft_mm, 2 * i + 2)
                for j in range(4):
                    ins = ts(H2T[i % 2][:, 4 + j, :], ps[:, 5, j * P:(j + 1) * P], A2[:, 4 + j:5 + j],
                             MODC[:, 2, 4 + j, 0:1], ALU.mult, ALU.add)
                give(ins, ft_dve)

            def choose(i):
                dve.wait_ge(lg_mm, i + 1)
                step(tt(RTW[:, 0:NE], ps[:, 6, 0:NE], ROWS[:, 0:NE], ALU.add))
                step(v.max(W(0, 8), RTW[:, 0:NE]))
                step(v.max_index(W(8, 8).bitcast(mybir.dt.uint32), W(0, 8), RTW[:, 0:NE]))
                give(ts(W(24), W(0), -1.0, None, ALU.mult), gneg)
                step(v.tensor_copy(W(32, 8), W(8, 8).bitcast(mybir.dt.uint32)))
                for k in range(TOPK):
                    step(ts(RTW[:, (4 + k) * NE:(5 + k) * NE], IOTA, W(32 + k), None, ALU.is_equal))
                step(tt(RTW[:, 3 * NE:4 * NE], RTW[:, 4 * NE:5 * NE], RTW[:, 5 * NE:6 * NE], ALU.add))
                step(tt(RTW[:, NE:2 * NE], RTW[:, 6 * NE:7 * NE], RTW[:, 7 * NE:8 * NE], ALU.add))
                give(tt(RTW[:, NE:2 * NE], RTW[:, NE:2 * NE], RTW[:, 3 * NE:4 * NE], ALU.add), route_m)

            def place(i):
                dve.wait_ge(rk_mm, i + 1)
                step(tt(RTW[:, 3 * NE:4 * NE], ps[:, 7, 0:NE], EBASE, ALU.add))
                step(tt(RTW[:, 2 * NE:3 * NE], RTW[:, 2 * NE:3 * NE], RTW[:, NE:2 * NE], ALU.add))
                for k in range(TOPK):
                    step(tt(RTW[:, 0:NE], RTW[:, (4 + k) * NE:(5 + k) * NE], RTW[:, 3 * NE:4 * NE], ALU.mult))
                    step(v.tensor_reduce(W(40 + k), RTW[:, 0:NE], X, ALU.add))
                dve.wait_ge(gexp, i + 1)
                step(v.reciprocal(W(26), W(25)))
                ts(PAIR[:, i * TOPK:(i + 1) * TOPK, 1], W(16, 4), W(26), None, ALU.mult)
                give(v.tensor_copy(SLOTI[:, i, :], W(40, 4)), slot_ready)
                dve.wait_ge(slot_ready, i + 1)

            for i in range(TT + 2):
                if 1 <= i <= TT:
                    fill_h2(i - 1)
                if i >= 2:
                    place(i - 2)
                if i < TT:
                    residual(i)
                if 1 <= i <= TT:
                    choose(i - 1)
            dve.wait_ge(cnt_mm, 1)
            v.memset(W(51), 0.0)
            v.tensor_reduce(W(50), ps[:, 7, 0:NE], X, ALU.max)
            step(v.tensor_copy(CNT[:, 0:NE], ps[:, 7, 0:NE]))
            v.tensor_copy(CNT[:, NE:NE + 1], W(51))
            give(v.tensor_copy(CNT[:, NE + 1:NE + 2], W(50)), cnt_ready)
            dve.wait_ge(list_mm, 1)
            v.memset(W(0), 0.0)
            v.tensor_copy(LGATE[:, :], ps[:, 6, NE * LCOL:2 * NE * LCOL])
            give(v.tensor_copy(LTOK[:, 0:NE * LCOL], ps[:, 6, 0:NE * LCOL]), list_ready)
            stage_end(dve, 6)

            dve.sem_inc(gu_evac, 4)
            dve.sem_inc(yt_ready, 2)

            def one(it, e, block, count, count_next):
                def times_sigmoid(w, half, m):
                    n = 4 * half + m
                    dve.wait_ge(sg_ready, it * 8 + n + 1)
                    tt(TG[:, m, 0:w], GA[:, m % 2, 0:w], SG[:, m % 2, 0:w], ALU.mult).then_inc(tg_step, 1)
                    dve.wait_ge(tg_step, it * 8 + n + 1)

                def body(w):
                    for half in range(2):
                        for m in range(4):
                            t = 8 * half + m
                            dve.wait_ge(gu_done, it * 16 + t + 1)
                            ts(GA[:, m % 2, 0:w], ps[:, m, 0:w], BGU[:, bass.ds(e * 16 + 4 * half + m, 1)], LIMIT,
                               ALU.add, ALU.min).then_inc(gu_evac, 1)
                            dve.wait_ge(gu_evac, it * 16 + 4 + t + 1)
                            if m:
                                times_sigmoid(w, half, m - 1)
                        times_sigmoid(w, half, 3)
                        for m in range(4):
                            t = 8 * half + 4 + m
                            n = 4 * half + m
                            dve.wait_ge(gu_done, it * 16 + t + 1)
                            ts(U1[:, 0:w], ps[:, m, 0:w], BGU[:, bass.ds(e * 16 + 8 + n, 1)], LIMIT + 1.0,
                               ALU.add, ALU.min).then_inc(gu_evac, 1)
                            dve.wait_ge(gu_evac, it * 16 + 4 + t + 1)
                            stt(out=HE[:, n, 0:w], in0=U1[:, 0:w], scalar=1.0 - LIMIT, in1=TG[:, m, 0:w], op0=ALU.max,
                                op1=ALU.mult).then_inc(he_ready, 1)
                            dve.wait_ge(he_ready, it * 8 + n + 1)
                    for d in range(DT):
                        dve.wait_ge(y_done, it * 8 + d + 1)
                        ts(YT[:, d, 0:w], ps[:, 4 + d % 2, 0:w], BDN[:, bass.ds(e * 8 + d, 1)], MODC[:, 4, d, 0:1],
                           ALU.add, ALU.mult).then_inc(yt_ready, 1)
                by_width(dve, count, BLOCKS, body)

            passes(dve, one)
            stage_end(dve, 7)

        @block.gpsimd
        def _(pool):
            g = nc.gpsimd
            for n in range(1, 6):
                stage_end(pool, n)
            g.memset(XSR[:, :, :], 0.0).then_inc(rows_init, 1)
            g.memset(LF[:, :, :], float(NOTOKEN)).then_inc(list_fill, 1)
            pool.wait_ge(list_fill, 1)
            pool.dma_start(list_d.rearrange("(p f) o -> p (f o)", p=P), LF[:, :, :].rearrange("p f o -> p (f o)")).then_inc(list_init, 16)
            pool.wait_ge(list_init, 16)
            for i in range(TT):
                pool.wait_ge(slot_ready, i + 1)
                for k in range(TOPK):
                    n = i * TOPK + k
                    g.indirect_dma_start(out=list_d, out_offset=bass.IndirectOffsetOnAxis(ap=SLOTI[:, i, k:k + 1], axis=0),
                                         in_=PAIR[:, n, :], in_offset=None).then_inc(list_out, 16)
            pool.wait_ge(list_out, 16 * PAIRS // P)
            lv = list_d.rearrange("(g r c) o -> g r (c o)", g=2, c=P)
            for h in range(2):
                pool.dma_start(JF[:, 2 * h * P:2 * (h + 1) * P], lv[h]).then_inc(list_in, 16)
            stage_end(pool, 6)

            pool.wait_ge(cnt_ready, 1)
            pool.wait_ge(rows_init, 1)
            pool.sem_inc(yr_free, 1)
            LAST_TOK = T - 1
            rows_due, results_due = pool.alloc_register("rows_due"), pool.alloc_register("results_due")
            pool.reg_mov(rows_due, 0)
            pool.reg_mov(results_due, 0)

            def gather(number, column, count):
                g.tensor_copy(IXG[:, :], LTOK[:, bass.ds(column, NB)]).then_inc(ix_step, 1)
                pool.wait_ge(ix_step, number * 2 + 1)
                pool.sem_inc(pool_mark, 1)

                def body(w):
                    for b in range(w // P):
                        g.indirect_dma_start(out=XSR[:, b, :], out_offset=None, in_=xn_d,
                                             in_offset=bass.IndirectOffsetOnAxis(ap=IXG[:, b:b + 1], axis=0),
                                             bounds_check=LAST_TOK, oob_is_err=False).then_inc(xs_in, 16)
                    pool.reg_add(rows_due, rows_due, 16 * (w // P))
                by_width(pool, count, BLOCKS, body)
                pool.wait_ge(xs_in, pool.snap(rows_due, min_val=16, max_val=16 * NB * (2 * NE + 2)))
                pool.sem_inc(rows_ready, 1)

            def one(it, e, block, count, count_next):
                pool.wait_ge(tp_done, it * 16 + 8)
                pool.sem_inc(pool_mark, 1)
                gather(it + 1, e * LCOL + NB if block else (e + 1) * LCOL, count if block else count_next)
                g.tensor_copy(IXS[:, :], LTOK[:, bass.ds(e * LCOL + NB * block, NB)]).then_inc(ix_step, 1)
                g.tensor_copy(GATES[:, :], LGATE[:, bass.ds(e * LCOL + NB * block, NB)]).then_inc(gates_ready, 1)
                pool.wait_ge(ix_step, it * 2 + 4)
                pool.wait_ge(tp_evac, it * 16 + 26)
                pool.sem_inc(pool_mark, 1)

                def scatter(w):
                    for b in range(w // P):
                        g.indirect_dma_start(out=out, out_offset=bass.IndirectOffsetOnAxis(ap=IXS[:, b:b + 1], axis=0),
                                             in_=YR[:, b, :], in_offset=None,
                                             bounds_check=LAST_TOK, oob_is_err=False, compute_op=ALU.add).then_inc(y_out, 16)
                    pool.reg_add(results_due, results_due, 16 * (w // P))
                by_width(pool, count, BLOCKS, scatter)
                pool.wait_ge(y_out, pool.snap(results_due, min_val=16, max_val=16 * NB * 2 * NE))
                pool.sem_inc(yr_free, 1)

            gather(0, 0, pool.value_load(CNT[0:1, 0:1], min_val=0, max_val=CAP))
            pool.sem_inc(ix_step, 1)
            passes(pool, one)
            stage_end(pool, 7)


_OUT = "out"


def kernel(**inputs):
    import concourse.bacc as bacc
    from concourse.bass_utils import run_bass_kernel_spmd

    v = {n: np.asarray(x) for n, x in inputs.items()}
    arrays = {**constants(), **layout(v)}
    nc = bacc.Bacc("TRN2", target_bir_lowering=False, num_devices=1)
    args = {n: nc.dram_tensor(n + "_dram", x.shape, mybir.dt.from_np(x.dtype), kind="ExternalInput").ap()
            for n, x in arrays.items()}
    out = nc.dram_tensor(_OUT, (T, D), F32, kind="ExternalOutput").ap()
    build(nc, args, out)
    r = run_bass_kernel_spmd(nc, [{n + "_dram": x for n, x in arrays.items()}], core_ids=[0])
    return r.results[0][_OUT].reshape(1, T, D)
```
